# Optimizing a Trainium2 kernel written in Bass

```python
import jax, jax.numpy as jnp
from jax import lax
import numpy as np
import math

D_MODEL = 1024
BATCH = 1
SEQ = 256
DEPTH = 1

D_MIX = 512
N_BRANCH = 3
GLA_HEADS = 4
GLA_DK = 64
GLA_DV = 128
GLA_RANK = 16
GLA_TAU = 16.0
GLA_CHUNK = 64
POOL_WINDOWS = (2, 4, 8, 16)
POOL_GROUPS = 4
POOL_GC = D_MIX // POOL_GROUPS
MOBA_HEADS = 8
MOBA_DH = D_MIX // MOBA_HEADS
MOBA_BLOCK = 256
MOBA_TOPK = 3
MOBA_QBLOCK = 128
D_FF = -(-8 * D_MODEL // (3 * 256)) * 256
EPS = 1e-6
NEG = -1e30

IN_SIZES = (GLA_HEADS * GLA_DK, GLA_HEADS * GLA_DK, GLA_HEADS * GLA_DV, GLA_RANK,
            GLA_HEADS * GLA_DV, D_MIX, D_MIX, D_MIX, D_MIX, N_BRANCH * D_MODEL)
D_IN = sum(IN_SIZES)


def rmsnorm(x, w):
    xf = x.astype(jnp.float32)
    y = xf * lax.rsqrt(jnp.mean(xf * xf, axis=-1, keepdims=True) + EPS)
    return (y * w.astype(jnp.float32)).astype(x.dtype)

def gla_mixer(q, k, v, g1, r, w_g2, b_g, norm_w):
    B, T, _ = q.shape
    H, DK, DV, C = GLA_HEADS, GLA_DK, GLA_DV, GLA_CHUNK
    NC = T // C
    f32 = jnp.float32
    qf = q.astype(f32).reshape(B, T, H, DK) * (DK ** -0.5)
    kf = k.astype(f32).reshape(B, T, H, DK)
    vf = v.astype(f32).reshape(B, T, H, DV)
    logit = (g1 @ w_g2 + b_g).astype(f32)
    log_a = (jax.nn.log_sigmoid(logit) / GLA_TAU).reshape(B, T, H, DK)

    def to_chunks(a):
        return a.reshape(B, NC, C, H, a.shape[-1]).transpose(1, 0, 3, 2, 4)

    causal = jnp.tril(jnp.ones((C, C), dtype=bool))

    def step(S, inp):
        qc, kc, vc, gc = inp
        bc = jnp.cumsum(gc, axis=2)
        diff = bc[:, :, :, None, :] - bc[:, :, None, :, :]
        decay = jnp.exp(jnp.where(causal[None, None, :, :, None], diff, NEG))
        attn = jnp.einsum('bhtd,bhsd,bhtsd->bhts', qc, kc, decay)
        o = (jnp.einsum('bhts,bhsv->bhtv', attn, vc)
             + jnp.einsum('bhtd,bhdv->bhtv', qc * jnp.exp(bc), S))
        b_last = bc[:, :, -1:, :]
        S = (jnp.exp(b_last[:, :, 0, :])[..., None] * S
             + jnp.einsum('bhsd,bhsv->bhdv', kc * jnp.exp(b_last - bc), vc))
        return S, o

    S0 = jnp.zeros((B, H, DK, DV), f32)
    _, o = lax.scan(step, S0, (to_chunks(qf), to_chunks(kf), to_chunks(vf), to_chunks(log_a)))
    o = o.transpose(1, 0, 3, 2, 4).reshape(B, T, H, DV)
    o = o * lax.rsqrt(jnp.mean(o * o, axis=-1, keepdims=True) + EPS) * norm_w.astype(f32)
    o = o.reshape(B, T, H * DV) * jax.nn.silu(r.astype(f32))
    return o.astype(q.dtype)

def pool_mixer(u, w_pool, scale):
    B, T, _ = u.shape
    f32 = jnp.float32
    uf = u.astype(f32).reshape(B, T, POOL_GROUPS, POOL_GC)
    cs = jnp.cumsum(uf, axis=1)
    t = jnp.arange(T)
    outs = []
    for gi, w in enumerate(POOL_WINDOWS):
        c = cs[:, :, gi]
        lag = jnp.pad(c, ((0, 0), (w, 0), (0, 0)))[:, :T]
        cnt = jnp.minimum(t + 1, w).astype(f32)[None, :, None]
        outs.append((c - lag) / cnt - uf[:, :, gi])
    p = jnp.stack(outs, axis=2)
    y = jnp.einsum('btgc,gcd->btgd', p, w_pool.astype(f32)).reshape(B, T, D_MIX)
    return (y * scale.astype(f32)).astype(u.dtype)

def moba_mixer(q, k, v):
    B, T, _ = q.shape
    H, DH, BLK, QB = MOBA_HEADS, MOBA_DH, MOBA_BLOCK, MOBA_QBLOCK
    NB = -(-T // BLK)
    NQ = T // QB
    KSEL = min(MOBA_TOPK, NB)
    f32 = jnp.float32
    qh = q.reshape(B, T, H, DH).transpose(0, 2, 1, 3)
    kh = k.reshape(B, T, H, DH).transpose(0, 2, 1, 3)
    vh = v.reshape(B, T, H, DH).transpose(0, 2, 1, 3)
    pad = NB * BLK - T
    kp = jnp.pad(kh, ((0, 0), (0, 0), (0, pad), (0, 0)))
    vp = jnp.pad(vh, ((0, 0), (0, 0), (0, pad), (0, 0)))
    kblk = kp.reshape(B, H, NB, BLK, DH)
    vblk = vp.reshape(B, H, NB, BLK, DH)
    kmean = jnp.mean(kblk.astype(f32), axis=3)
    gate = jnp.einsum('bhtd,bhnd->bhtn', qh.astype(f32), kmean)
    tblk = jnp.arange(T) // BLK
    past = jnp.arange(NB)[None, :] < tblk[:, None]
    gate = jnp.where(past[None, None], gate, NEG)
    _, idx = lax.top_k(gate, KSEL)
    valid = jnp.arange(KSEL)[None, :] < tblk[:, None]
    slopes = (2.0 ** (-8.0 * (jnp.arange(H) + 1) / H)).astype(f32)
    scale = DH ** -0.5
    hi = jnp.arange(H)[:, None, None]

    def one_block(i):
        b = i // NQ
        t0 = (i % NQ) * QB
        qb = lax.dynamic_slice(qh, (b, 0, t0, 0), (1, H, QB, DH))[0]
        ib = lax.dynamic_slice(idx, (b, 0, t0, 0), (1, H, QB, KSEL))[0]
        vm = lax.dynamic_slice(valid, (t0, 0), (QB, KSEL))
        kg = kblk[b][hi, ib]
        vg = vblk[b][hi, ib]
        own0 = (t0 // BLK) * BLK
        ko = lax.dynamic_slice(kp, (b, 0, own0, 0), (1, H, BLK, DH))[0]
        vo = lax.dynamic_slice(vp, (b, 0, own0, 0), (1, H, BLK, DH))[0]
        tq = t0 + jnp.arange(QB)
        s_sel = ib[..., None] * BLK + jnp.arange(BLK)
        s_own = own0 + jnp.arange(BLK)
        sc_sel = (jnp.einsum('hqd,hqkjd->hqkj', qb, kg).astype(f32) * scale
                  - slopes[:, None, None, None] * (tq[None, :, None, None] - s_sel).astype(f32))
        sc_sel = jnp.where(vm[None, :, :, None], sc_sel, NEG)
        sc_own = (jnp.einsum('hqd,hjd->hqj', qb, ko).astype(f32) * scale
                  - slopes[:, None, None] * (tq[:, None] - s_own[None, :]).astype(f32)[None])
        sc_own = jnp.where((s_own[None, :] <= tq[:, None])[None], sc_own, NEG)
        sc = jnp.concatenate([sc_sel.reshape(H, QB, KSEL * BLK), sc_own], axis=-1)
        p = jax.nn.softmax(sc, axis=-1).astype(v.dtype)
        p_sel = p[..., :KSEL * BLK].reshape(H, QB, KSEL, BLK)
        p_own = p[..., KSEL * BLK:]
        return (jnp.einsum('hqkj,hqkjd->hqd', p_sel, vg)
                + jnp.einsum('hqj,hjd->hqd', p_own, vo))

    out = lax.map(one_block, jnp.arange(B * NQ))
    return out.reshape(B, NQ, H, QB, DH).transpose(0, 1, 3, 2, 4).reshape(B, T, H * DH)

def first_inputs(seed: int = 0) -> dict:
    key = jax.random.key(seed)
    ks = jax.random.split(key, 20)
    f32 = jnp.float32

    def nrm(k, shape, fan_in):
        return jax.random.normal(k, shape, f32) * (fan_in ** -0.5)

    def gain(k, shape):
        return 1.0 + 0.05 * jax.random.normal(k, shape, f32)

    L = DEPTH
    return {
        "x": jax.random.normal(ks[0], (BATCH, SEQ, D_MODEL), f32),
        "norm_mix_pre": gain(ks[1], (L, D_MODEL)),
        "w_in": nrm(ks[2], (L, D_MODEL, D_IN), D_MODEL),
        "gla_w_g2": nrm(ks[3], (L, GLA_RANK, GLA_HEADS * GLA_DK), GLA_RANK),
        "gla_b_g": 0.1 * jax.random.normal(ks[4], (L, GLA_HEADS * GLA_DK), f32),
        "gla_norm": gain(ks[5], (L, GLA_DV)),
        "pool_w": nrm(ks[6], (L, POOL_GROUPS, POOL_GC, POOL_GC), POOL_GC),
        "pool_scale": gain(ks[7], (L, D_MIX)),
        "w_branch_a": nrm(ks[8], (L, D_MIX, D_MODEL), D_MIX),
        "w_branch_b": nrm(ks[9], (L, D_MIX, D_MODEL), D_MIX),
        "w_branch_c": nrm(ks[10], (L, D_MIX, D_MODEL), D_MIX),
        "w_out": nrm(ks[11], (L, D_MODEL, D_MODEL), D_MODEL),
        "norm_mix_post": gain(ks[12], (L, D_MODEL)),
        "norm_ffn_pre": gain(ks[13], (L, D_MODEL)),
        "ffn_w_gate": nrm(ks[14], (L, D_MODEL, D_FF), D_MODEL),
        "ffn_w_up": nrm(ks[15], (L, D_MODEL, D_FF), D_MODEL),
        "ffn_w_down": nrm(ks[16], (L, D_FF, D_MODEL), D_FF),
        "norm_ffn_post": gain(ks[17], (L, D_MODEL)),
    }

def first_block(x, norm_mix_pre, w_in, gla_w_g2, gla_b_g, gla_norm, pool_w, pool_scale,
              w_branch_a, w_branch_b, w_branch_c, w_out, norm_mix_post, norm_ffn_pre,
              ffn_w_gate, ffn_w_up, ffn_w_down, norm_ffn_post):
    B, T, D = x.shape
    splits = [int(s) for s in np.cumsum(IN_SIZES)[:-1]]
    for l in range(DEPTH):
        h = rmsnorm(x, norm_mix_pre[l])
        proj = h @ w_in[l]
        gq, gk, gv, gg1, gr, pu, mq, mk, mv, gates = jnp.split(proj, splits, axis=-1)
        ya = gla_mixer(gq, gk, gv, gg1, gr, gla_w_g2[l], gla_b_g[l], gla_norm[l]) @ w_branch_a[l]
        yb = pool_mixer(pu, pool_w[l], pool_scale[l]) @ w_branch_b[l]
        yc = moba_mixer(mq, mk, mv) @ w_branch_c[l]
        gs = jax.nn.sigmoid(gates).reshape(B, T, N_BRANCH, D)
        mixed = gs[:, :, 0] * ya + gs[:, :, 1] * yb + gs[:, :, 2] * yc
        x = x + rmsnorm(mixed @ w_out[l], norm_mix_post[l])
        h = rmsnorm(x, norm_ffn_pre[l])
        f = (jax.nn.silu(h @ ffn_w_gate[l]) * (h @ ffn_w_up[l])) @ ffn_w_down[l]
        x = x + rmsnorm(f, norm_ffn_post[l])
    return x


D_FF_2 = 2816
HEAD_DIM = 64
NSA_HEADS = 8
NSA_KV_GROUPS = 2
NSA_HPG = NSA_HEADS // NSA_KV_GROUPS
CMP_BLOCK = 32
CMP_STRIDE = 16
CMP_HIDDEN = 256
SEL_BLOCK = 64
SEL_TOP_N = 16
SEL_Q_BLOCK = 64
WINDOW = 512
WIN_Q_BLOCK = 128
FOX_HEADS = 8
FOX_Q_BLOCK = 128
MEM_LEN = 256
MEM_HEADS = 4
MEM_HEAD_DIM = D_MODEL // MEM_HEADS
NUM_BUCKETS = 32
MAX_DISTANCE = 128
RMS_EPS = 1e-6
NEG_INF = -1e30
FORCE_BONUS = 1e4

NSA_Q = NSA_HEADS * HEAD_DIM
NSA_KV = NSA_KV_GROUPS * HEAD_DIM
FOX_W = FOX_HEADS * HEAD_DIM
IN_SPLITS = (NSA_Q, NSA_KV, NSA_KV, NSA_KV, NSA_KV, NSA_KV, NSA_KV, 3 * NSA_HEADS,
             FOX_W, FOX_W, FOX_W, FOX_HEADS, D_MODEL, D_MODEL)
IN_WIDTH = NSA_Q + 6 * NSA_KV + 3 * NSA_HEADS + 3 * FOX_W + FOX_HEADS + 2 * D_MODEL


def rmsnorm_2(x, g):
    x32 = x.astype(jnp.float32)
    y = x32 * lax.rsqrt(jnp.mean(x32 * x32, axis=-1, keepdims=True) + RMS_EPS)
    return (y * g.astype(jnp.float32)).astype(x.dtype)

def swiglu(h, w_gate, w_up, w_down):
    return (jax.nn.silu(h @ w_gate) * (h @ w_up)) @ w_down

def split_cols(z, sizes):
    return jnp.split(z, np.cumsum(sizes)[:-1].tolist(), axis=-1)

def t5_bucket(dist):
    n = jnp.maximum(dist, 0)
    exact = NUM_BUCKETS // 2
    nf = jnp.maximum(n, 1).astype(jnp.float32)
    large = exact + (jnp.log(nf / exact) / math.log(MAX_DISTANCE / exact)
                     * (NUM_BUCKETS - exact)).astype(jnp.int32)
    large = jnp.minimum(large, NUM_BUCKETS - 1)
    return jnp.where(n < exact, n, large)

def masked_softmax(s, mask):
    s = jnp.where(mask, s.astype(jnp.float32), NEG_INF)
    p = jax.nn.softmax(s, axis=-1)
    return jnp.where(mask, p, 0.0)

def cmp_sel_overlap(n_cmp, n_sel):
    c0 = np.arange(n_cmp)[:, None] * CMP_STRIDE
    s0 = np.arange(n_sel)[None, :] * SEL_BLOCK
    ov = np.clip(np.minimum(c0 + CMP_BLOCK, s0 + SEL_BLOCK) - np.maximum(c0, s0), 0, None)
    return jnp.asarray(ov / CMP_STRIDE, dtype=jnp.float32)

def compress(kv, pos, w1, w2):
    b, s, g, d = kv.shape
    n_chunks = s // CMP_STRIDE
    r = CMP_BLOCK // CMP_STRIDE
    nc = n_chunks - r + 1
    chunks = kv.reshape(b, n_chunks, CMP_STRIDE, g, d)
    blocks = jnp.concatenate([chunks[:, i:i + nc] for i in range(r)], axis=2)
    blocks = blocks + pos[None, None, :, None, :]
    flat = blocks.transpose(0, 1, 3, 2, 4).reshape(b, nc, g, CMP_BLOCK * d)
    return jax.nn.gelu(flat @ w1) @ w2

def nsa_attention(q, k_c, v_c, k_s, v_s, k_w, v_w, g_nsa, rel_bias_table,
                  cmp_pos_k, cmp_pos_v, cmp_k_w1, cmp_k_w2, cmp_v_w1, cmp_v_w2):
    b, s = q.shape[:2]
    G, J, D = NSA_KV_GROUPS, NSA_HPG, HEAD_DIM
    qg = q.reshape(b, s, G, J, D) * (D ** -0.5)
    t = jnp.arange(s)
    tbl = rel_bias_table.reshape(NUM_BUCKETS, G, J)

    kc = compress(k_c, cmp_pos_k, cmp_k_w1, cmp_k_w2)
    vc = compress(v_c, cmp_pos_v, cmp_v_w1, cmp_v_w2)
    nc = kc.shape[1]
    c_end = jnp.arange(nc) * CMP_STRIDE + CMP_BLOCK - 1
    dist_c = t[:, None] - c_end[None, :]
    bias_c = tbl[t5_bucket(dist_c)].transpose(2, 3, 0, 1)
    s_c = jnp.einsum('bsgjd,bcgd->bgjsc', qg, kc) + bias_c
    p_c = masked_softmax(s_c, dist_c >= 0)
    o_c = jnp.einsum('bgjsc,bcgd->bsgjd', p_c.astype(vc.dtype), vc)

    n_sel = s // SEL_BLOCK
    top_n = min(SEL_TOP_N, n_sel)
    imp = jnp.einsum('bgjsc,cn->bgsn', p_c, cmp_sel_overlap(nc, n_sel))
    blk = jnp.arange(n_sel)[None, :]
    cur = (t // SEL_BLOCK)[:, None]
    forced = (blk == 0) | (blk == cur) | (blk == cur - 1)
    imp = jnp.where(blk * SEL_BLOCK <= t[:, None],
                    imp + jnp.where(forced, FORCE_BONUS, 0.0), NEG_INF)
    _, sel_idx = lax.top_k(imp, top_n)

    kb = k_s.reshape(b, n_sel, SEL_BLOCK, G, D).transpose(0, 3, 1, 2, 4)
    vb = v_s.reshape(b, n_sel, SEL_BLOCK, G, D).transpose(0, 3, 1, 2, 4)
    nq = s // SEL_Q_BLOCK
    q_blocks = qg.reshape(b, nq, SEL_Q_BLOCK, G, J, D).transpose(1, 0, 3, 4, 2, 5)
    idx_blocks = sel_idx.reshape(b, G, nq, SEL_Q_BLOCK, top_n).transpose(2, 0, 1, 3, 4)
    bi = jnp.arange(b)[:, None, None, None]
    gi = jnp.arange(G)[None, :, None, None]
    gi5 = jnp.arange(G)[None, :, None, None, None]
    r = jnp.arange(SEL_BLOCK)

    def sel_block(args):
        qb, ib, start = args
        kg = kb[bi, gi, ib]
        vg = vb[bi, gi, ib]
        tq = start + jnp.arange(SEL_Q_BLOCK)
        pos = ib[..., None] * SEL_BLOCK + r
        dist = tq[None, None, :, None, None] - pos
        bias = tbl[t5_bucket(dist), gi5].transpose(0, 1, 5, 2, 3, 4)
        sc = jnp.einsum('bgjqd,bgqnrd->bgjqnr', qb, kg) + bias
        flat = top_n * SEL_BLOCK
        p = masked_softmax(sc.reshape(b, G, J, SEL_Q_BLOCK, flat),
                           (dist >= 0).reshape(b, G, 1, SEL_Q_BLOCK, flat))
        p = p.reshape(b, G, J, SEL_Q_BLOCK, top_n, SEL_BLOCK).astype(vg.dtype)
        return jnp.einsum('bgjqnr,bgqnrd->bqgjd', p, vg)

    o_s = lax.map(sel_block, (q_blocks, idx_blocks, jnp.arange(nq) * SEL_Q_BLOCK))
    o_s = o_s.transpose(1, 0, 2, 3, 4, 5).reshape(b, s, G, J, D)

    nw = s // WIN_Q_BLOCK
    span = WINDOW + WIN_Q_BLOCK
    kpad = jnp.pad(k_w, ((0, 0), (WINDOW, 0), (0, 0), (0, 0)))
    vpad = jnp.pad(v_w, ((0, 0), (WINDOW, 0), (0, 0), (0, 0)))
    win_idx = (jnp.arange(nw) * WIN_Q_BLOCK)[:, None] + jnp.arange(span)[None, :]
    kwin = kpad[:, win_idx]
    vwin = vpad[:, win_idx]
    qw = qg.reshape(b, nw, WIN_Q_BLOCK, G, J, D)
    dist_w = jnp.arange(WIN_Q_BLOCK)[:, None] + WINDOW - jnp.arange(span)[None, :]
    bias_w = tbl[t5_bucket(dist_w)].transpose(2, 3, 0, 1)[:, :, None]
    mask_w = ((dist_w >= 0) & (dist_w < WINDOW))[None] & (win_idx >= WINDOW)[:, None, :]
    s_w = jnp.einsum('bnqgjd,bnkgd->bgjnqk', qw, kwin) + bias_w
    p_w = masked_softmax(s_w, mask_w)
    o_w = jnp.einsum('bgjnqk,bnkgd->bnqgjd', p_w.astype(vwin.dtype), vwin).reshape(b, s, G, J, D)

    g = jax.nn.sigmoid(g_nsa).reshape(b, s, 3, G, J)[..., None]
    o = g[:, :, 0] * o_c + g[:, :, 1] * o_s + g[:, :, 2] * o_w
    return o.reshape(b, s, NSA_Q)

def forgetting_attention(q, k, v, f_logit):
    b, s, h, d = q.shape
    c = jnp.cumsum(jax.nn.log_sigmoid(f_logit.astype(jnp.float32)), axis=1).transpose(0, 2, 1)
    nb = s // FOX_Q_BLOCK
    qb = (q * (d ** -0.5)).reshape(b, nb, FOX_Q_BLOCK, h, d).transpose(1, 0, 3, 2, 4)
    cb = c.reshape(b, h, nb, FOX_Q_BLOCK).transpose(2, 0, 1, 3)
    kpos = jnp.arange(s)

    def block(args):
        qi, ci, start = args
        sc = jnp.einsum('bhqd,bkhd->bhqk', qi, k).astype(jnp.float32) + ci[..., None] - c[:, :, None, :]
        mask = (start + jnp.arange(FOX_Q_BLOCK))[:, None] >= kpos[None, :]
        p = masked_softmax(sc, mask)
        return jnp.einsum('bhqk,bkhd->bqhd', p.astype(v.dtype), v)

    o = lax.map(block, (qb, cb, jnp.arange(nb) * FOX_Q_BLOCK))
    return o.transpose(1, 0, 2, 3, 4).reshape(b, s, h * d)

def hybrid_mixer(h, w_in, b_forget, rel_bias_table, cmp_pos_k, cmp_pos_v, cmp_k_w1, cmp_k_w2,
                 cmp_v_w1, cmp_v_w2, w_up_nsa, w_up_fox, w_out):
    b, s, _ = h.shape
    (q_n, k_c, v_c, k_s, v_s, k_w, v_w, g_nsa, q_f, k_f, v_f, f_logit,
     gate_a, gate_b) = split_cols(h @ w_in, IN_SPLITS)
    kvh = lambda z: z.reshape(b, s, NSA_KV_GROUPS, HEAD_DIM)
    o_nsa = nsa_attention(q_n, kvh(k_c), kvh(v_c), kvh(k_s), kvh(v_s), kvh(k_w), kvh(v_w), g_nsa,
                          rel_bias_table, cmp_pos_k, cmp_pos_v, cmp_k_w1, cmp_k_w2, cmp_v_w1, cmp_v_w2)
    fh = lambda z: z.reshape(b, s, FOX_HEADS, HEAD_DIM)
    o_fox = forgetting_attention(fh(q_f), fh(k_f), fh(v_f), f_logit + b_forget)
    y = jax.nn.sigmoid(gate_a) * (o_nsa @ w_up_nsa) + jax.nn.sigmoid(gate_b) * (o_fox @ w_up_fox)
    return y @ w_out

def memory_cross_attention(h, mem_n, w_q, w_kv, w_o):
    b, s, _ = h.shape
    q = (h @ w_q).reshape(b, s, MEM_HEADS, MEM_HEAD_DIM) * (MEM_HEAD_DIM ** -0.5)
    k, v = jnp.split(mem_n @ w_kv, 2, axis=-1)
    k = k.reshape(b, -1, MEM_HEADS, MEM_HEAD_DIM)
    v = v.reshape(b, -1, MEM_HEADS, MEM_HEAD_DIM)
    p = jax.nn.softmax(jnp.einsum('bshd,bmhd->bhsm', q, k).astype(jnp.float32), axis=-1)
    o = jnp.einsum('bhsm,bmhd->bshd', p.astype(v.dtype), v).reshape(b, s, D_MODEL)
    return o @ w_o

def second_inputs(seed: int = 0) -> dict:
    key = jax.random.key(seed)
    ks = iter(jax.random.split(key, 40))
    nrm = lambda shape, scale: jax.random.normal(next(ks), shape, jnp.float32) * scale
    gain = lambda shape: 1.0 + nrm(shape, 0.02)
    L = DEPTH
    return {
        'x': nrm((BATCH, SEQ, D_MODEL), 1.0),
        'mem': nrm((BATCH, MEM_LEN, D_MODEL), 1.0),
        'rel_bias_table': nrm((NUM_BUCKETS, NSA_HEADS), 0.5),
        'ffn1_norm': gain((L, D_MODEL)),
        'ffn1_w_gate': nrm((L, D_MODEL, D_FF_2), D_MODEL ** -0.5),
        'ffn1_w_up': nrm((L, D_MODEL, D_FF_2), D_MODEL ** -0.5),
        'ffn1_w_down': nrm((L, D_FF_2, D_MODEL), D_FF_2 ** -0.5),
        'mix_norm': gain((L, D_MODEL)),
        'mix_w_in': nrm((L, D_MODEL, IN_WIDTH), D_MODEL ** -0.5),
        'mix_b_forget': 2.0 + nrm((L, FOX_HEADS), 0.5),
        'cmp_pos_k': nrm((L, CMP_BLOCK, HEAD_DIM), 0.1),
        'cmp_pos_v': nrm((L, CMP_BLOCK, HEAD_DIM), 0.1),
        'cmp_k_w1': nrm((L, CMP_BLOCK * HEAD_DIM, CMP_HIDDEN), (CMP_BLOCK * HEAD_DIM) ** -0.5),
        'cmp_k_w2': nrm((L, CMP_HIDDEN, HEAD_DIM), 2.0 * CMP_HIDDEN ** -0.5),
        'cmp_v_w1': nrm((L, CMP_BLOCK * HEAD_DIM, CMP_HIDDEN), (CMP_BLOCK * HEAD_DIM) ** -0.5),
        'cmp_v_w2': nrm((L, CMP_HIDDEN, HEAD_DIM), 2.0 * CMP_HIDDEN ** -0.5),
        'w_up_nsa': nrm((L, NSA_Q, D_MODEL), NSA_Q ** -0.5),
        'w_up_fox': nrm((L, FOX_W, D_MODEL), FOX_W ** -0.5),
        'mix_w_out': nrm((L, D_MODEL, D_MODEL), D_MODEL ** -0.5),
        'mem_q_norm': gain((L, D_MODEL)),
        'mem_kv_norm': gain((L, D_MODEL)),
        'mem_w_q': nrm((L, D_MODEL, D_MODEL), D_MODEL ** -0.5),
        'mem_w_kv': nrm((L, D_MODEL, 2 * D_MODEL), D_MODEL ** -0.5),
        'mem_w_o': nrm((L, D_MODEL, D_MODEL), D_MODEL ** -0.5),
        'ffn2_norm': gain((L, D_MODEL)),
        'ffn2_w_gate': nrm((L, D_MODEL, D_FF_2), D_MODEL ** -0.5),
        'ffn2_w_up': nrm((L, D_MODEL, D_FF_2), D_MODEL ** -0.5),
        'ffn2_w_down': nrm((L, D_FF_2, D_MODEL), D_FF_2 ** -0.5),
        'final_norm': gain((D_MODEL,)),
    }

def second_block(x, mem, rel_bias_table, ffn1_norm, ffn1_w_gate, ffn1_w_up, ffn1_w_down,
              mix_norm, mix_w_in, mix_b_forget, cmp_pos_k, cmp_pos_v, cmp_k_w1, cmp_k_w2,
              cmp_v_w1, cmp_v_w2, w_up_nsa, w_up_fox, mix_w_out, mem_q_norm, mem_kv_norm,
              mem_w_q, mem_w_kv, mem_w_o, ffn2_norm, ffn2_w_gate, ffn2_w_up, ffn2_w_down,
              final_norm):
    for l in range(DEPTH):
        x = x + 0.5 * swiglu(rmsnorm_2(x, ffn1_norm[l]), ffn1_w_gate[l], ffn1_w_up[l], ffn1_w_down[l])
        x = x + hybrid_mixer(rmsnorm_2(x, mix_norm[l]), mix_w_in[l], mix_b_forget[l], rel_bias_table,
                             cmp_pos_k[l], cmp_pos_v[l], cmp_k_w1[l], cmp_k_w2[l], cmp_v_w1[l],
                             cmp_v_w2[l], w_up_nsa[l], w_up_fox[l], mix_w_out[l])
        x = x + memory_cross_attention(rmsnorm_2(x, mem_q_norm[l]), rmsnorm_2(mem, mem_kv_norm[l]),
                                       mem_w_q[l], mem_w_kv[l], mem_w_o[l])
        x = x + 0.5 * swiglu(rmsnorm_2(x, ffn2_norm[l]), ffn2_w_gate[l], ffn2_w_up[l], ffn2_w_down[l])
    return rmsnorm_2(x, final_norm)


def setup_inputs(seed=0):
    out = dict(first_inputs(seed))
    for name, value in second_inputs(seed + 1).items():
        if name != "x":
            out[name + "_2"] = value
    return out


def reference(
    x, norm_mix_pre, w_in, gla_w_g2, gla_b_g, gla_norm, pool_w, pool_scale, w_branch_a,
    w_branch_b, w_branch_c, w_out, norm_mix_post, norm_ffn_pre, ffn_w_gate, ffn_w_up,
    ffn_w_down, norm_ffn_post, mem_2, rel_bias_table_2, ffn1_norm_2, ffn1_w_gate_2, ffn1_w_up_2,
    ffn1_w_down_2, mix_norm_2, mix_w_in_2, mix_b_forget_2, cmp_pos_k_2, cmp_pos_v_2, cmp_k_w1_2,
    cmp_k_w2_2, cmp_v_w1_2, cmp_v_w2_2, w_up_nsa_2, w_up_fox_2, mix_w_out_2, mem_q_norm_2,
    mem_kv_norm_2, mem_w_q_2, mem_w_kv_2, mem_w_o_2, ffn2_norm_2, ffn2_w_gate_2, ffn2_w_up_2,
    ffn2_w_down_2, final_norm_2,
):
    x = first_block(
        x, norm_mix_pre, w_in, gla_w_g2, gla_b_g, gla_norm, pool_w, pool_scale, w_branch_a,
        w_branch_b, w_branch_c, w_out, norm_mix_post, norm_ffn_pre, ffn_w_gate, ffn_w_up,
        ffn_w_down, norm_ffn_post,
    )
    return second_block(
        x, mem_2, rel_bias_table_2, ffn1_norm_2, ffn1_w_gate_2, ffn1_w_up_2, ffn1_w_down_2,
        mix_norm_2, mix_w_in_2, mix_b_forget_2, cmp_pos_k_2, cmp_pos_v_2, cmp_k_w1_2,
        cmp_k_w2_2, cmp_v_w1_2, cmp_v_w2_2, w_up_nsa_2, w_up_fox_2, mix_w_out_2, mem_q_norm_2,
        mem_kv_norm_2, mem_w_q_2, mem_w_kv_2, mem_w_o_2, ffn2_norm_2, ffn2_w_gate_2,
        ffn2_w_up_2, ffn2_w_down_2, final_norm_2,
    )


_drawn_inputs = setup_inputs


def setup_inputs(seed=0):
    import zlib

    import numpy as np

    out = dict(_drawn_inputs(seed))
    spreads = {}
    factors = {'gla_b_g': 2.933,
     'ffn1_norm_2': 8.0,
     'mix_norm_2': 8.0,
     'cmp_pos_k_2': 8.0,
     'cmp_pos_v_2': 3.42,
     'mem_q_norm_2': 8.0,
     'mem_kv_norm_2': 8.0,
     'ffn2_norm_2': 23.991,
     'final_norm_2': 8.378}
    for name, (base, spread) in spreads.items():
        noise = np.random.default_rng([zlib.crc32(name.encode()), seed]).standard_normal(out[name].shape)
        drawn = base * np.exp(spread * noise) if base else spread * noise
        out[name] = __import__('jax').numpy.asarray(drawn.astype(out[name].dtype))
    for name, factor in factors.items():
        out[name] = (out[name] * factor).astype(out[name].dtype)
    return out
```

```python
from contextlib import ExitStack

import numpy as np

import concourse.bass as bass
from concourse import mybir

F32 = mybir.dt.float32
F32R = mybir.dt.float32r
U8 = mybir.dt.uint8
ALU = mybir.AluOpType
ACT = mybir.ActivationFunctionType
AX = mybir.AxisListType.X

NEG = -1e30
EPS = 1e-6
T = 256
D = 1024
FF = 2816
UNIT = 1024
NRAW = 4
NSPL = 4
AHEAD = 2
START, ROOM = 16512, 212832


def _cols(*spans):
    return np.concatenate([np.arange(a, b) for a, b in spans])


def weight_chunks():
    out = []

    def add(name, weight, cols, rows):
        out.append((name, weight, cols, rows))

    def halves(name, weight, rows):
        for n in range(2):
            add(f"{name}{n}", weight, _cols((512 * n, 512 * n + 512)), rows)

    def ffn(name, gate, up, down):
        for c in range(11):
            add(f"{name}gu{c}", (gate, up), _cols((256 * c, 256 * c + 256)), D)
        halves(f"{name}dn", down, FF)

    for name, a, b in (("qk", 0, 512), ("g1", 1024, 1040), ("gv", 512, 1024), ("gr", 1040, 1552),
                       ("pu", 1552, 2064), ("mq", 2064, 2576), ("mk", 2576, 3088), ("mv", 3088, 3600)):
        add(name, "w_in", _cols((a, b)), D)
    for n in range(6):
        add(f"gt{n}", "w_in", _cols((3600 + 512 * n, 4112 + 512 * n)), D)
    halves("br0", "w_branch_a", 512)
    halves("br1", "w_branch_b", 512)
    halves("br2", "w_branch_c", 512)
    halves("wo", "w_out", D)
    ffn("f0", "ffn_w_gate", "ffn_w_up", "ffn_w_down")
    ffn("f1", "ffn1_w_gate_2", "ffn1_w_up_2", "ffn1_w_down_2")
    w = "mix_w_in_2"
    add("kv", w, _cols((512, 576), (512, 576), (576, 640), (576, 640),
                       (640, 704), (640, 704), (704, 768), (704, 768)), D)
    add("gf", w, _cols((1280, 1304), (2840, 2848)), D)
    add("qn", w, _cols(*[(64 * (4 * g + i), 64 * (4 * g + i) + 64) for i in range(4) for g in range(2)]), D)
    add("ksw", w, _cols((768, 896), (1024, 1152)), D)
    add("vsw", w, _cols((896, 1024), (1152, 1280)), D)
    add("qf", w, _cols((1304, 1816)), D)
    add("kf", w, _cols((1816, 2328)), D)
    add("vf", w, _cols((2328, 2840)), D)
    for n in range(4):
        add(f"gg{n}", w, _cols((2848 + 512 * n, 3360 + 512 * n)), D)
    halves("up0", "w_up_nsa_2", 512)
    halves("up1", "w_up_fox_2", 512)
    halves("mo", "mix_w_out_2", D)
    for n in range(4):
        add(f"mkv{n}", "mem_w_kv_2", _cols((512 * n, 512 * n + 512)), D)
    halves("cq", "mem_w_q_2", D)
    halves("co", "mem_w_o_2", D)
    ffn("f2", "ffn2_w_gate_2", "ffn2_w_up_2", "ffn2_w_down_2")
    return out


def unit_plan():
    units, chunks, at = [], {}, 0
    for name, weight, cols, rows in weight_chunks():
        n = len(cols) * (2 if isinstance(weight, tuple) else 1)
        kt = min(rows // 128, max(1, UNIT // n))
        ids = []
        for k0 in range(0, rows // 128, kt):
            k = min(kt, rows // 128 - k0)
            ids.append(len(units))
            units.append((at, k, n, k0))
            at += 128 * k * n
        chunks[name] = ids
    return units, chunks, at


MASKS = [1, 2, 4, 8, 16, 32, 64]
C_ID, C_CM, C_INV, C_ROW, C_RST = 0, 128, 512, 576, 577
C_ALL = 577 + 256


def constants():
    f = np.float32
    c = np.zeros((128, C_ALL), f)
    c[:, C_ID:C_ID + 128] = np.eye(128, dtype=f)
    q = np.arange(128)[:, None]
    c[:, C_CM:C_CM + 128] = np.where(np.arange(128)[None] <= q, 0, NEG)
    c[:, C_CM + 128:C_CM + 384] = np.where(np.arange(256)[None] <= q + 128, 0, NEG)
    for g in range(4):
        c[:, C_INV + 16 * g:C_INV + 16 * g + 16] = 1.0 / np.minimum(np.arange(16) + 1, 2 << g).astype(f)
    c[:, C_ROW] = (np.arange(128) >= 31)
    c[:, C_RST:C_RST + 256] = (np.arange(256) % 64 != 0)
    t = np.arange(128)
    s = t[:, None]
    masks = [(s // (2 * m) == t // (2 * m)) & (s % (2 * m) < m) & (t % (2 * m) >= m) for m in MASKS]
    masks = np.stack(masks + [s == t], 1).astype(f).reshape(128, 8 * 128)
    slope = (2.0 ** (-8.0 * (np.arange(8) + 1) / 8)).astype(f)
    parts = []
    for qb in range(2):
        tq = np.arange(128)[:, None, None] + 128 * qb
        k = np.arange(128 * (qb + 1))[None, None]
        b = -(slope[None, :, None] * (tq - k).astype(f))
        parts.append(np.where(k <= tq, b, NEG).astype(f).reshape(128, -1))
    alibi = np.concatenate(parts, 1)
    hot = np.zeros((33, 512), f)
    dist = 255 - np.arange(512)
    n = np.maximum(dist, 0)
    large = 16 + (np.log(np.maximum(n, 1).astype(f) / f(16)) / f(np.log(8.0)) * f(16)).astype(np.int32)
    bucket = np.where(n < 16, n, np.minimum(large, 31))
    for u in range(512):
        hot[bucket[u] if dist[u] >= 0 else 32, u] = 1
    sel = np.zeros((8, 8, 128), f)
    for h in range(8):
        sel[h, h] = -1
    return {"c_cst": c, "c_masks": masks, "c_alibi": alibi, "c_hot": hot, "c_sel": sel.reshape(8, 1024)}


COLS = {}
for _n, _w in (("norm_mix_pre", 8), ("norm_ffn_pre", 8), ("pool_scale", 4), ("gla_b_g", 2), ("ffn1_norm_2", 8),
               ("mix_norm_2", 8), ("mem_q_norm_2", 8), ("mem_kv_norm_2", 8), ("ffn2_norm_2", 8), ("mix_b_forget_2", 1)):
    COLS[_n] = (sum(w for _, w in COLS.values()), _w)
N_COLS = sum(w for _, w in COLS.values())


class Queue:

    def __init__(self, sem):
        self.sem, self.n, self.seen, self.items = sem, 0, {}, []

    def wait(self, after):
        for sem, v in after:
            if self.seen.get(sem.name, 0) < v:
                self.seen[sem.name] = v
                self.items.append((sem, v))

    def put(self, fn, *after):
        self.wait(after)
        self.n += 1
        self.items.append((fn, None))
        return self.last

    @property
    def last(self):
        return (self.sem, self.n)

    def run(self, eng):
        for a, v in self.items:
            if v is not None:
                eng.wait_ge(a, v)
            else:
                a(eng).then_inc(self.sem, 1)


class DmaQueue:

    def __init__(self):
        self.items, self.seen = [], {}

    def put(self, sem, count, out, in_, *after):
        for s, v in after:
            if self.seen.get(s.name, 0) < v:
                self.seen[s.name] = v
                self.items.append((s, v, None, None))
        count[sem.name] = count.get(sem.name, 0) + 16
        self.items.append((sem, None, out, in_))
        return (sem, count[sem.name])

    def run(self, eng):
        for s, v, out, in_ in self.items:
            if v is not None:
                eng.wait_ge(s, v)
            else:
                eng.dma_start(out, in_).then_inc(s, 16)


class Slot:
    def __init__(self, ap):
        self.ap, self.free = ap, []


class Ring:
    def __init__(self, aps):
        self.slots, self.i = [Slot(a) for a in aps], 0

    def get(self):
        self.i += 1
        return self.slots[(self.i - 1) % len(self.slots)]


class Split:

    def __init__(self, hi, lo, first, n):
        self.hi, self.lo, self.first, self.tok = hi, lo, first, [None] * n

    def h(self, k):
        return self.hi[:, self.first + k, :]

    def l(self, k):
        return self.lo[:, self.first + k, :]


def build(nc, io):
    with ExitStack() as ctx:
        def sem(name):
            return ctx.enter_context(nc.semaphore(name))

        P, A, V = Queue(sem("s_pe")), Queue(sem("s_act")), Queue(sem("s_dve"))
        G = Queue(sem("s_pool"))
        SP, AD, GD = DmaQueue(), DmaQueue(), DmaQueue()
        cnt = {}
        S_RAW = [sem(f"s_raw{i}") for i in range(NRAW)]
        s_out = sem("s_out")

        ctx.enter_context(nc.sbuf_tensor("slab", [128, ROOM // 4], F32))
        top = [START]

        def at(name, shape, dt, off):
            return nc.alloc_sbuf_tensor_at(name, shape, dt, offset=off)

        def fixed(name, shape, dt=F32):
            size = int(np.prod(shape[1:])) * (1 if dt == U8 else 4)
            t = at(name, shape, dt, top[0])
            top[0] += (size + 31) // 32 * 32
            return t

        raw = [fixed(f"raw{i}", [128, UNIT]) for i in range(NRAW)]
        whi = [fixed(f"whi{i}", [128, UNIT], F32R) for i in range(NSPL)]
        wlo = [fixed(f"wlo{i}", [128, UNIT], F32R) for i in range(NSPL)]
        x = fixed("x", [128, 2, D])
        hT_hi = fixed("hT_hi", [128, 8, T], F32R)
        hT_lo = fixed("hT_lo", [128, 8, T], F32R)
        cst = fixed("cst", [128, C_ALL])
        cols = fixed("cols", [128, N_COLS])
        row = fixed("row", [128, D])
        sm = fixed("sm", [128, 512])
        arena = top[0]
        limit = START + ROOM
        ident = cst[:, C_ID:C_ID + 128]

        class Phase:

            def __init__(self, tag):
                self.tag, self.off = tag, arena

            def new(self, name, shape, dt=F32, off=None):
                size = (int(np.prod(shape[1:])) * (1 if dt == U8 else 4) + 31) // 32 * 32
                o = self.off if off is None else off
                t = at(f"{self.tag}_{name}", shape, dt, o)
                if off is None:
                    self.off += size
                assert max(self.off, o + size) <= limit, (name, self.off - limit)
                return t

        sm_at = [0]

        def small(n):
            if sm_at[0] + n > 512:
                sm_at[0] = 0
            sm_at[0] += n
            return sm[:, sm_at[0] - n:sm_at[0]]

        banks = [ctx.enter_context(nc.psum_tensor(f"ps{i}", [128, 512], F32)) for i in range(8)]
        GR, SR = Ring(banks[0:4]), Ring(banks[4:8])

        def load(q, name, out, in_, *after):
            return q.put(sem("l_" + name), cnt, out, in_, *after)

        def bcast(ap, n):
            return bass.AP(tensor=ap.tensor, offset=ap.offset, ap=[[0, 128], [1, n]])

        xin = io["x"].rearrange("a (k p) d -> p (a k) d", p=128)
        t_x = [load(SP, f"x{t}", x[:, t, :], xin[:, t, :]) for t in range(2)]
        t_cst = load(AD, "cst", cst[:, :], io["c_cst"])
        t_cols = load(AD, "cols", cols[:, :], io["cols"])

        def col(name, i):
            return cols[:, COLS[name][0] + i:COLS[name][0] + i + 1]



        units, chunks, _ = unit_plan()
        raw_tok, split_tok, used_tok = {}, {}, {}
        nxt = [0]

        def fetch(u, *after):
            if u < len(units):
                off, k, n, _ = units[u]
                src = bass.AP(tensor=io["wflat"].tensor, offset=off, ap=[[k * n, 128], [1, k * n]])
                raw_tok[u] = SP.put(S_RAW[u % NRAW], cnt, raw[u % NRAW][:, 0:k * n], src, *after)

        for u in range(NRAW):
            fetch(u)

        def split_to(u):
            while nxt[0] <= min(u, len(units) - 1):
                i = nxt[0]
                _, k, n, _ = units[i]
                r, h, l = (b[i % m][:, 0:k * n] for b, m in ((raw, NRAW), (whi, NSPL), (wlo, NSPL)))
                pe = [used_tok[i - NSPL]] if i >= NSPL else []
                ta = A.put(lambda e, r=r, h=h: e.activation(h, r, ACT.Copy), raw_tok[i], *pe)
                tv = V.put(lambda e, r=r, h=h, l=l: e.tensor_tensor(l, r, h.bitcast(F32), ALU.subtract), ta)
                split_tok[i] = tv
                fetch(i + NRAW, tv)
                nxt[0] += 1

        tasks = []

        def tick():
            for t in list(tasks):
                if next(t, "end") == "end":
                    tasks.remove(t)

        def drain(*which):
            which = which or tuple(tasks)
            while any(t in tasks for t in which):
                tick()

        def spawn(gen):
            tasks.append(gen)
            return gen

        def gemm_a(name, xs, evac):
            ids = chunks[name]
            slots = [GR.get(), GR.get()]
            for j, u in enumerate(ids):
                _, kt, n, k0 = units[u]
                split_to(u + AHEAD)
                hi = whi[u % NSPL][:, 0:kt * n].rearrange("p (k n) -> p k n", n=n)
                lo = wlo[u % NSPL][:, 0:kt * n].rearrange("p (k n) -> p k n", n=n)
                toks = [xs.tok[k0 + k] for k in range(kt)] + [split_tok[u]]
                if j == 0:
                    toks += slots[0].free + slots[1].free

                def mm(e, first=j == 0, last=j == len(ids) - 1, kt=kt, n=n, k0=k0, hi=hi, lo=lo):
                    for k in range(kt):
                        for t in range(2):
                            o = slots[t].ap[:, 0:n]
                            xh = xs.h(k0 + k)[:, t * 128:t * 128 + 128]
                            xl = xs.l(k0 + k)[:, t * 128:t * 128 + 128]
                            e.matmul(o, xh, hi[:, k, :], start=first and k == 0, stop=False)
                            e.matmul(o, xh, lo[:, k, :], start=False, stop=False)
                            r = e.matmul(o, xl, hi[:, k, :], start=False, stop=last and k == kt - 1)
                    return r

                tp = used_tok[u] = P.put(mm, *toks)
                if j < len(ids) - 1:
                    tick()
            for t in range(2):
                slots[t].free = evac(t, slots[t].ap, tp)
            tick()

        def gemm_b(name, xs, evac):
            ids = chunks[name]
            n = units[ids[0]][2]
            slots = [GR.get() for _ in range(n // 256)]
            for j, u in enumerate(ids):
                _, kt, n, k0 = units[u]
                split_to(u + AHEAD)
                hi = whi[u % NSPL][:, 0:kt * n].rearrange("p (k n) -> p k n", n=n)
                lo = wlo[u % NSPL][:, 0:kt * n].rearrange("p (k n) -> p k n", n=n)
                toks = [xs.tok[k0 + k] for k in range(kt)] + [split_tok[u]]
                if j == 0:
                    for s in slots:
                        toks += s.free

                def mm(e, first=j == 0, last=j == len(ids) - 1, kt=kt, n=n, k0=k0, hi=hi, lo=lo):
                    for f in range(n // 128):
                        o = slots[f // 2].ap[:, 256 * (f % 2):256 * (f % 2) + 256]
                        c = slice(128 * f, 128 * f + 128)
                        for k in range(kt):
                            e.matmul(o, hi[:, k, c], xs.h(k0 + k), start=first and k == 0 and f % 2 == 0,
                                     stop=False, skip_group_check=True)
                            e.matmul(o, lo[:, k, c], xs.h(k0 + k), start=False, stop=False, skip_group_check=True)
                            r = e.matmul(o, hi[:, k, c], xs.l(k0 + k), start=False,
                                         stop=last and k == kt - 1, skip_group_check=True)
                    return r

                tp = used_tok[u] = P.put(mm, *toks)
                if j < len(ids) - 1:
                    tick()
            for i, s in enumerate(slots):
                s.free = evac(i, s.ap, tp)
            tick()

        def to_split(dst, d0, n, src, after, scale=None):
            for f in range(0, n, 2):
                s = SR.get()

                def tr(e, f=f, s=s):
                    for i in range(2):
                        for t in range(2):
                            r = e.transpose(s.ap[:, 256 * i + 128 * t:256 * i + 128 * t + 128],
                                            src(t)[:, 128 * (f + i):128 * (f + i) + 128], ident)
                    return r

                tp = P.put(tr, t_cst, *s.free, *after)
                s.free = [split_psum(dst, d0 + f, s.ap, tp, scale and [scale(f), scale(f + 1)])]

        def split_psum(dst, k, ps, tp, scale=None):
            p2 = ps[:, :].rearrange("p (i t) -> p i t", i=2)
            f = dst.first + k
            if scale is None:
                h, l = dst.hi[:, f:f + 2, :], dst.lo[:, f:f + 2, :]
                ta = A.put(lambda e: e.activation(h, p2, ACT.Copy), tp)
                tv = V.put(lambda e: e.tensor_tensor(l, p2, h.bitcast(F32), ALU.subtract), ta)
            else:
                for i in range(2):
                    h, c, pi = dst.hi[:, f + i, :], scale[i], p2[:, i, :]
                    ta = A.put(lambda e, h=h, c=c, pi=pi: e.activation(h, pi, ACT.Identity, scale=c), tp, t_cols)
                for i in range(2):
                    h, l, c, pi = dst.hi[:, f + i, :], dst.lo[:, f + i, :], scale[i], p2[:, i, :]
                    tv = V.put(lambda e, h=h, l=l, c=c, pi=pi: e.scalar_tensor_tensor(
                        out=l, in0=pi, scalar=c, in1=h.bitcast(F32), op0=ALU.mult, op1=ALU.subtract), ta)
            dst.tok[k] = dst.tok[k + 1] = tv
            return tv

        def rstd(ss, n, mean, *after):
            v, y, w = small(n), small(n), small(n)
            t = V.put(lambda e: e.tensor_scalar(v, ss, mean, EPS, ALU.mult, ALU.add), *after)
            t = A.put(lambda e: e.activation(w, v, ACT.Sqrt), t)
            t = V.put(lambda e: e.reciprocal(y, w), t)
            t = V.put(lambda e: e.tensor_tensor(w, v, y, ALU.mult), t)
            t = V.put(lambda e: e.tensor_tensor(w, w, y, ALU.mult), t)
            t = V.put(lambda e: e.tensor_scalar(w, w, -0.5, 1.5, ALU.mult, ALU.add), t)
            t = V.put(lambda e: e.tensor_tensor(y, y, w, ALU.mult), t)
            return y, t

        def rms_scaled(src, xn, after):
            ss = small(2)
            for t in range(2):
                ta = A.put(lambda e, t=t: e.activation(xn[:, t, :], src[:, t, :], ACT.Square,
                                                       accum_out=ss[:, t:t + 1]), after[t])
            r, tr = rstd(ss, 2, 1.0 / D, ta)
            return [V.put(lambda e, t=t: e.tensor_scalar(xn[:, t, :], src[:, t, :], r[:, t:t + 1], None, ALU.mult), tr)
                    for t in range(2)]

        def norm_t(src, xn, after, norm, dst, d0=0):
            tt = rms_scaled(src, xn, after)
            to_split(dst, d0, 8, lambda t: xn[:, t, :], tt, lambda f: col(norm, f))

        def everything():
            return [q.last for q in (P, A, V) if q.n]

        def residual_rms(name, xs, fb, w_tok, x_tok):
            ss = small(4)
            tok = {}
            for n in range(2):
                def evac(t, ps, tp, n=n):
                    a = A.put(lambda e: e.activation(fb[:, t, 512 * n:512 * n + 512], ps[:, :], ACT.Copy), tp)
                    a = A.put(lambda e: e.activation(ps[:, :], ps[:, :], ACT.Square,
                                                     accum_out=ss[:, 2 * n + t:2 * n + t + 1]), a)
                    tok[n, t] = a
                    return [a]
                gemm_a(f"{name}{n}", xs, evac)
            s2 = small(2)
            tv = V.put(lambda e: e.tensor_tensor(s2, ss[:, 0:2], ss[:, 2:4], ALU.add), tok[1, 1])
            r, tr = rstd(s2, 2, 1.0 / D, tv)
            out = []
            for t in range(2):
                a = V.put(lambda e, t=t: e.scalar_tensor_tensor(
                    out=fb[:, t, :], in0=fb[:, t, :], scalar=r[:, t:t + 1], in1=row[:, :],
                    op0=ALU.mult, op1=ALU.mult), tr, w_tok)
                out.append(V.put(lambda e, t=t: e.tensor_tensor(x[:, t, :], x[:, t, :], fb[:, t, :], ALU.add),
                                 a, x_tok[t]))
            return out

        def residual(name, xs, factor, x_tok):
            out = [None, None]
            for n in range(2):
                def evac(t, ps, tp, n=n):
                    xx = x[:, t, 512 * n:512 * n + 512]
                    out[t] = V.put(lambda e: e.scalar_tensor_tensor(
                        out=xx, in0=ps[:, :], scalar=factor, in1=xx, op0=ALU.mult, op1=ALU.add), tp, x_tok[t])
                    return [out[t]]
                gemm_a(f"{name}{n}", xs, evac)
            return out

        hT = Split(hT_hi, hT_lo, 0, 8)

        def ffn(tag, norm, x_tok, finish):
            ph = Phase(tag)
            xn = ph.new("xn", [128, 2, D])
            hid_hi = ph.new("hid_hi", [128, 22, T], F32R)
            hid_lo = ph.new("hid_lo", [128, 22, T], F32R)
            sg = [ph.new(f"sg{i}", [128, 2, 256]) for i in range(2)]
            hh = [ph.new(f"hh{i}", [128, 2, 256]) for i in range(2)]
            fb = ph.new("fb", [128, 2, D])
            hid = Split(hid_hi, hid_lo, 0, 22)
            for q in (A, V):
                q.wait(everything())
            norm_t(x, xn, x_tok, norm, hT)
            sg_free, hh_free = [[], []], [[], []]

            def turn(c, tv):
                yield
                to_split(hid, 2 * c, 2, lambda t: hh[c % 2][:, t, :], tv)
                hh_free[c % 2] = [P.last]

            for c in range(11):
                tv = [None, None]

                def evac(t, ps, tp, c=c, tv=tv):
                    a = A.put(lambda e: e.activation(sg[c % 2][:, t, :], ps[:, 0:256], ACT.Silu),
                              tp, *sg_free[c % 2])
                    tv[t] = V.put(lambda e: e.tensor_tensor(hh[c % 2][:, t, :], sg[c % 2][:, t, :], ps[:, 256:512],
                                                            ALU.mult), a, *hh_free[c % 2])
                    return [tv[t]]

                gemm_a(f"{tag}gu{c}", hT, evac)
                sg_free[c % 2] = [tv[1]]
                spawn(turn(c, tv))
            drain()
            return finish(f"{tag}dn", hid, fb)

        def softmax_block(ph_P, mx, sums, heads, L, after):
            nm = small(heads)
            t = V.put(lambda e: e.tensor_scalar(nm, mx, -1.0, None, ALU.mult), *after)
            for h in range(heads):
                t = A.put(lambda e, h=h: e.activation(ph_P[:, h, 0:L], ph_P[:, h, 0:L], ACT.Exp,
                                                      bias=nm[:, h:h + 1], accum_out=sums[:, h:h + 1]), t)
            return t

        def attention(Pb, PT, score, bias, value, after, vtok, out, prior=(), order=(0, 2, 4, 6, 1, 3, 5, 7)):
            p_free = list(prior)
            for qb in range(2):
                L = 128 * (qb + 1)
                mx, sums, rec = small(8), small(8), small(8)
                per = 512 // L
                for g in range(0, 8, per):
                    hs = order[g:g + per]
                    s = SR.get()

                    def mm(e, s=s, hs=hs, qb=qb, L=L):
                        for i, h in enumerate(hs):
                            r = score(e, s.ap[:, i * L:i * L + L], h, qb, L)
                        return r

                    tp = P.put(mm, *s.free, *after)
                    for i, h in enumerate(hs):
                        tv = V.put(lambda e, s=s, i=i, h=h, qb=qb, L=L, mx=mx: e.tensor_tensor_reduce(
                            Pb[:, h, 0:L], s.ap[:, i * L:i * L + L], bias(qb, h), 1.0, -3.0e38,
                            ALU.add, ALU.max, mx[:, h:h + 1]), tp, *p_free)
                    s.free = [tv]
                    if g % 4 == 2 or per == 4:
                        yield
                te = softmax_block(Pb, mx, sums, 8, L, [tv])
                tr = V.put(lambda e, rec=rec, sums=sums: e.reciprocal(rec, sums), te)
                yield
                blocks = [(h, k) for h in range(8) for k in range(qb + 1)]
                for b in range(0, len(blocks), 4):
                    s = SR.get()

                    def tr4(e, s=s, b=b, blocks=blocks):
                        for i, (h, k) in enumerate(blocks[b:b + 4]):
                            r = e.transpose(s.ap[:, 128 * i:128 * i + 128], Pb[:, h, 128 * k:128 * k + 128], ident)
                        return r

                    tp = P.put(tr4, te, *s.free)
                    if b % 8 == 0:
                        tc = A.put(lambda e, s=s, b=b: e.activation(
                            PT[:, b:b + 4, :], s.ap[:, :].rearrange("p (i t) -> p i t", i=4), ACT.Copy), tp)
                    else:
                        tc = V.put(lambda e, s=s, b=b: e.tensor_copy(
                            PT[:, b:b + 4, :], s.ap[:, :].rearrange("p (i t) -> p i t", i=4)), tp)
                    s.free = [tc]
                p_free = [tp]
                ends = [A.last, V.last]
                yield
                s = SR.get()

                def pv(e, s=s, qb=qb):
                    for h in range(8):
                        for k in range(qb + 1):
                            r = e.matmul(s.ap[:, 64 * h:64 * h + 64], PT[:, h * (qb + 1) + k, :], value(h, k),
                                         start=k == 0, stop=k == qb)
                    return r

                tp = P.put(pv, *ends, *vtok, *s.free)
                s.free = out(qb, s.ap[:, :].rearrange("p (h d) -> p h d", h=8), rec, [tp, tr])
                yield

        def spread(ap, n):
            return ap.unsqueeze(2).to_broadcast([128, ap.shape[1], n])

        m1 = Phase("m1")
        br_hi, br_lo = m1.new("br_hi", [128, 8, T], F32R), m1.new("br_lo", [128, 8, T], F32R)
        gates = m1.new("gates", [128, 2, 3072])
        r1 = m1.off
        xn = m1.new("xn", [128, 2, D])
        m1.new("r1b", [128, 2, D])
        gv, gr = m1.new("gv", [128, 2, 512]), m1.new("gr", [128, 2, 512])
        mq, mk = m1.new("mq", [128, 4, T]), m1.new("mk", [128, 4, T])
        mv = m1.new("mv", [128, 2, 512])
        pu = m1.new("pu", [128, 4, 16 + T])
        gqk_off = m1.off
        gqk = m1.new("gqk", [128, 4, T])
        bcum = m1.new("bcum", [128, 2, T])
        r2 = m1.off
        lE = m1.new("lE", [128, 8, T])
        lQ = m1.new("lQ", [128, 8, T])
        lK = m1.new("lK", [128, 8, T])
        m1.new("r2pad", [128, D])
        acc_off = m1.off
        acc = m1.new("acc", [128, 3, 4, 128])
        msk = m1.new("msk", [128, 8, 128], U8)
        wg2 = m1.new("wg2", [128, 256])
        wpl = m1.new("wpl", [128, 4, 128])
        g1 = m1.new("g1", [128, 2, 16])
        g1T = m1.new("g1T", [128, 256])
        gnw = m1.new("gnw", [128, 128])
        t1 = m1.new("t1", [128, 4, 272], off=r1)
        t2 = m1.new("t2", [128, 4, 272], off=r1 + 4352)
        pp = m1.new("pp", [128, 4, T], off=r1 + 8704)
        mixed = m1.new("mixed", [128, 2, D], off=r1)
        mtmp = m1.new("mtmp", [128, 2, 512], off=r1 + 8192)
        lmn = m1.new("lmn", [128, 2, T], off=acc_off)
        lab = m1.new("lab", [128, 2, T], off=acc_off + 2048)
        yc = m1.new("yc", [128, 2, 512], off=gqk_off)
        Pb = m1.new("Pb", [128, 8, T], off=r2)
        PT = m1.new("PT", [128, 16, 128], off=r2 + 8192)
        fb1 = m1.new("fb", [128, 2, D], off=r2)
        mskf = m1.new("mskf", [128, D], off=r2)
        alibi = m1.new("alibi", [128, 8 * 384], off=r2 + 16384)

        t_msk = load(AD, "msk", mskf[:, :], io["c_masks"])
        t_msk = V.put(lambda e: e.tensor_copy(msk[:, :, :], mskf[:, :].rearrange("p (l t) -> p l t", l=8)), t_msk)
        t_wg2 = load(AD, "wg2", wg2[0:16, :], io["gla_w_g2"].rearrange("a r c -> (a r) c"))
        t_wpl = load(AD, "wpl", wpl[:, :, :], io["pool_w"].rearrange("a g c d -> c (a g) d"))
        t_gnw = load(AD, "gnw", gnw[:, :], bcast(io["gla_norm"], 128))
        t_row = load(AD, "row", row[:, :], bcast(io["norm_mix_post"], D))

        norm_t(x, xn, t_x, "norm_mix_pre", hT)
        done = {}

        def evac_gqk(i, ps, tp):
            o = gqk[:, 2 * i:2 * i + 2, :]
            p2 = ps[:, :].rearrange("p (i t) -> p i t", i=2)
            done["gqk", i] = A.put(lambda e: e.activation(o, p2, ACT.Copy, scale=0.125 if i == 0 else 1.0), tp)
            return [done["gqk", i]]

        br = Split(br_hi, br_lo, 0, 8)
        brc = Split(hT_hi, hT_lo, 0, 4)
        first = {}

        def gla():
            s1 = SR.get()

            def tr(e):
                for t in range(2):
                    r = e.transpose(s1.ap[0:16, 128 * t:128 * t + 128], g1[:, t, :], ident)
                return r

            tp = P.put(tr, first["g1"], *s1.free)
            tv = V.put(lambda e: e.tensor_copy(g1T[0:16, :], s1.ap[0:16, 0:256]), tp)
            s1.free = [tv]
            yield
            s2 = SR.get()

            def lg(e):
                for f in range(2):
                    r = e.matmul(s2.ap[:, 256 * f:256 * f + 256], wg2[0:16, 128 * f:128 * f + 128], g1T[0:16, :],
                                 start=True, stop=True)
                return r

            tp = P.put(lg, tv, t_wg2, *s2.free)
            for f in range(2):
                z = s2.ap[:, 256 * f:256 * f + 256]
                ta = A.put(lambda e, f=f, z=z: e.activation(lab[:, f, :], z, ACT.Abs, bias=col("gla_b_g", f)), tp, t_cols)
            for f in range(2):
                z = s2.ap[:, 256 * f:256 * f + 256]
                tv = V.put(lambda e, f=f, z=z: e.tensor_scalar(lmn[:, f, :], z, col("gla_b_g", f), 0.0,
                                                               ALU.add, ALU.min), ta, t_cols)
            s2.free = [ta, tv]
            ta = A.put(lambda e: e.activation(lab[:, :, :], lab[:, :, :], ACT.Exp, scale=-1.0), ta)
            ta = A.put(lambda e: e.activation(lab[:, :, :], lab[:, :, :], ACT.Ln, bias=1.0), ta)
            tv = V.put(lambda e: e.tensor_tensor(lmn[:, :, :], lmn[:, :, :], lab[:, :, :], ALU.subtract), ta, tv)
            for f in range(2):
                ts = V.put(lambda e, f=f: e.tensor_tensor_scan(bcum[:, f, :], cst[:, C_RST:C_RST + 256], lmn[:, f, :],
                                                               0.0, ALU.mult, ALU.add), tv, t_cst)
            tz = V.put(lambda e: e.memset(acc[:, :, :, :], 0.0), ts)
            yield
            free_l = []
            for pr in range(2):
                b = bcum[:, pr, :]
                for i, m in enumerate(MASKS):
                    bv = b.rearrange("p (n c) -> p n c", c=2 * m)
                    ev = lE[:, i, :].rearrange("p (n c) -> p n c", c=2 * m)
                    nb = T // (2 * m)
                    ref = bv[:, :, m - 1:m].to_broadcast([128, nb, m])
                    tv = V.put(lambda e, bv=bv, ev=ev, ref=ref, m=m: e.tensor_tensor(
                        ev[:, :, 0:m], ref, bv[:, :, 0:m], ALU.subtract), ts, *free_l)
                    if m < 64:
                        tv = V.put(lambda e, bv=bv, ev=ev, ref=ref, m=m: e.tensor_tensor(
                            ev[:, :, m:2 * m], bv[:, :, m:2 * m], ref, ALU.subtract), ts)
                    else:
                        tv = V.put(lambda e, bv=bv, ev=ev, m=m: e.tensor_copy(
                            ev[:, :, m:2 * m], bv[:, :, m:2 * m]), ts)
                sb0 = small(1)
                t0 = V.put(lambda e, b=b, sb0=sb0: e.tensor_tensor(sb0, b[:, 63:64], b[:, 127:128], ALU.add), ts)
                V.put(lambda e, b=b: e.tensor_scalar(lE[:, 7, 64:128], b[:, 64:128], -1.0, b[:, 127:128],
                                                     ALU.mult, ALU.add), ts)
                V.put(lambda e, b=b: e.tensor_copy(lE[:, 7, 128:192], b[:, 128:192]), ts)
                V.put(lambda e, b=b: e.tensor_scalar(lE[:, 7, 192:256], b[:, 192:256], b[:, 191:192], None, ALU.add), ts)
                tv = V.put(lambda e, b=b, sb0=sb0: e.tensor_scalar(lE[:, 7, 0:64], b[:, 0:64], -1.0, sb0,
                                                                   ALU.mult, ALU.add), t0)
                ta = A.put(lambda e: e.activation(lE[:, :, :], lE[:, :, :], ACT.Exp, scale=1.0 / 16), tv)
                yield
                for dst, src in ((lQ, gqk[:, pr, :]), (lK, gqk[:, 2 + pr, :])):
                    wide = src.unsqueeze(1).to_broadcast([128, 8, T])
                    tq = V.put(lambda e, dst=dst, wide=wide: e.tensor_tensor(dst[:, :, :], wide, lE[:, :, :], ALU.mult),
                               ta, done["gqk", 0], done["gqk", 1], *free_l)
                yield
                for par in range(2):
                    pa = slice(64 * par, 64 * par + 64)
                    h = 2 * pr + par
                    for j in range(2):
                        for half in range(2):
                            s = SR.get()

                            def lv(e, s=s, pa=pa, j=j, half=half, pr=pr):
                                for i in range(4):
                                    l = 4 * half + i
                                    w = slice(128 * j, 128 * j + 128)
                                    kk, qq = (lK[pa, l, w], lQ[pa, l, w]) if l < 7 else (gqk[pa, 2 + pr, w], gqk[pa, pr, w])
                                    r = e.matmul(s.ap[:, 128 * i:128 * i + 128], kk, qq, start=True, stop=True)
                                return r

                            tp = P.put(lv, tq, *s.free)
                            for i in range(4):
                                tv = V.put(lambda e, s=s, i=i, j=j, h=h, half=half: e.copy_predicated(
                                    acc[:, j, h, :], msk[:, 4 * half + i, :], s.ap[:, 128 * i:128 * i + 128]), tp, tz, t_msk, tv)
                            s.free = [tv]
                        yield
                    s = SR.get()
                    tp = P.put(lambda e, s=s, pa=pa: e.matmul(s.ap[:, 0:128], lK[pa, 7, 0:128], lQ[pa, 7, 128:256],
                                                              start=True, stop=True), tq, *s.free)
                    tv = A.put(lambda e, s=s, h=h: e.activation(acc[:, 2, h, :], s.ap[:, 0:128], ACT.Copy), tp, tz)
                    s.free = [tv]
                free_l = [tp]
            done["levels"] = tp
            ends = [A.last, V.last]
            yield
            for j in range(2):
                s = SR.get()

                def ov(e, s=s, j=j):
                    for h in range(4):
                        o = s.ap[:, 128 * h:128 * h + 128]
                        if j:
                            e.matmul(o, acc[:, 2, h, :], gv[:, 0, 128 * h:128 * h + 128], start=True, stop=False)
                        r = e.matmul(o, acc[:, j, h, :], gv[:, j, 128 * h:128 * h + 128], start=j == 0, stop=True)
                    return r

                tp = P.put(ov, *ends, first["gv"], *s.free)
                ss = small(4)
                for h in range(4):
                    ta = A.put(lambda e, s=s, h=h, j=j, ss=ss: e.activation(
                        lE[:, h, 0:128], s.ap[:, 128 * h:128 * h + 128], ACT.Square, accum_out=ss[:, h:h + 1]),
                        tp, done["levels"])
                r, tr = rstd(ss, 4, 1.0 / 128, ta)
                o3 = s.ap[:, :].rearrange("p (h d) -> p h d", h=4)
                tmp = lK[:, 2 * j:2 * j + 2, :].rearrange("p a (b d) -> p (a b) d", d=128)
                tv = V.put(lambda e, o3=o3, r=r, tmp=tmp: e.tensor_tensor(tmp, o3, spread(r, 128), ALU.mult), tr, done["levels"])
                s.free = [tv]
                g4 = gr[:, j, :].rearrange("p (h d) -> p h d", h=4)
                tv = V.put(lambda e, g4=g4, tmp=tmp: e.tensor_tensor(g4, tmp, g4, ALU.mult), tv, first["gr"])
            yield
            to_split(br, 0, 4, lambda t: gr[:, t, :], [tv])
            done["gla"] = [A.last, V.last, P.last]

        def pool():
            t0 = done["pu"]
            z = V.put(lambda e: e.memset(t1[:, :, 0:16], 0.0), *everything())
            z = V.put(lambda e: e.memset(t2[:, :, 0:16], 0.0))
            t = V.put(lambda e: e.tensor_tensor(t1[:, :, 1:272], pu[:, :, 1:272], pu[:, :, 0:271], ALU.add), z, *t0)
            t = V.put(lambda e: e.tensor_tensor(t2[:, 1:4, 3:272], t1[:, 1:4, 3:272], t1[:, 1:4, 1:270], ALU.add), t)
            yield
            t = V.put(lambda e: e.tensor_tensor(t1[:, 2:4, 7:272], t2[:, 2:4, 7:272], t2[:, 2:4, 3:268], ALU.add), t)
            t = V.put(lambda e: e.tensor_tensor(t2[:, 3, 15:272], t1[:, 3, 15:272], t1[:, 3, 7:264], ALU.add), t)
            inv = small(64)
            for g in range(4):
                src = (t1, t2)[g % 2]
                V.put(lambda e, g=g, src=src: e.scalar_tensor_tensor(
                    out=pp[:, g, :], in0=src[:, g, 16:272], scalar=1.0 / (2 << g), in1=pu[:, g, 16:272],
                    op0=ALU.mult, op1=ALU.subtract), t)
                t3 = V.put(lambda e, g=g, src=src: e.tensor_tensor(
                    inv[:, 16 * g:16 * g + 16], src[:, g, 16:32], cst[:, C_INV + 16 * g:C_INV + 16 * g + 16], ALU.mult), t)
            yield
            for g in range(4):
                t = V.put(lambda e, g=g: e.tensor_tensor(pp[:, g, 0:16], inv[:, 16 * g:16 * g + 16], pu[:, g, 16:32],
                                                         ALU.subtract), t3)
            for g in range(0, 4, 2):
                s = SR.get()

                def pm(e, s=s, g=g):
                    for i in range(2):
                        r = e.matmul(s.ap[:, 256 * i:256 * i + 256], wpl[:, g + i, :], pp[:, g + i, :], start=True, stop=True)
                    return r

                tp = P.put(pm, t, t_wpl, *s.free)
                s.free = [split_psum(br, 4 + g, s.ap, tp, [col("pool_scale", g), col("pool_scale", g + 1)])]
            done["pool"] = [P.last]

        def moba():
            t_alibi = load(GD, "alibi", alibi[:, :], io["c_alibi"], *done["gla"])

            def score(e, ps, h, qb, L):
                pa = slice(64 * (h % 2), 64 * (h % 2) + 64)
                return e.matmul(ps, mq[pa, h // 2, 128 * qb:128 * qb + 128], mk[pa, h // 2, 0:L], start=True, stop=True)

            def bias(qb, h):
                o, L = (0, 128) if qb == 0 else (1024, 256)
                return alibi[:, o + L * h:o + L * h + L]

            def out(qb, ps, rec, after):
                o = yc[:, qb, :].rearrange("p (h d) -> p h d", h=8)
                t = V.put(lambda e: e.tensor_tensor(o, ps, spread(rec, 64), ALU.mult), *after, *done["gla"])
                done["yc"] = t
                return [t]

            yield from attention(Pb, PT, score, bias, lambda h, k: mv[:, k, 64 * h:64 * h + 64],
                                 [done["mq"], done["mk"], t_alibi], [done["mv"]], out, done["gla"])
        gemm_b("qk", hT, evac_gqk)

        def keep(key, out, func=ACT.Copy, scale=1.0):
            def evac(t, ps, tp):
                o = out(t)
                n = o.shape[-1]
                first[key] = A.put(lambda e: e.activation(o, ps[:, 0:n], func, scale=scale), tp)
                return [first[key]]
            return evac

        gemm_a("g1", hT, keep("g1", lambda t: g1[:, t, :]))
        gemm_a("gv", hT, keep("gv", lambda t: gv[:, t, :]))
        t_gla = spawn(gla())
        tgr = []

        def evac_gr(t, ps, tp):
            a = A.put(lambda e: e.activation(gr[:, t, :], ps[:, :], ACT.Silu), tp)
            g4 = gr[:, t, :].rearrange("p (h d) -> p h d", h=4)
            first["gr"] = V.put(lambda e: e.tensor_tensor(
                g4, g4, gnw[:, :].unsqueeze(1).to_broadcast([128, 4, 128]), ALU.mult), a, t_gnw)
            return [a]

        gemm_a("gr", hT, evac_gr)

        z_pu = V.put(lambda e: e.memset(pu[:, :, 0:16], 0.0))
        done["pu"] = [z_pu]

        def evac_pu(i, ps, tp):
            p2 = ps[:, :].rearrange("p (i t) -> p i t", i=2)
            a = A.put(lambda e: e.activation(pu[:, 2 * i:2 * i + 2, 16:272], p2, ACT.Copy), tp)
            done["pu"].append(a)
            return [a]

        def keep_b(key, out, scale=1.0):
            def evac(i, ps, tp):
                p2 = ps[:, :].rearrange("p (i t) -> p i t", i=2)
                done[key] = A.put(lambda e: e.activation(out[:, 2 * i:2 * i + 2, :], p2, ACT.Copy, scale=scale), tp)
                return [done[key]]
            return evac

        gemm_b("pu", hT, evac_pu)
        spawn(pool())
        gemm_b("mq", hT, keep_b("mq", mq, 0.125))
        gemm_b("mk", hT, keep_b("mk", mk))

        def evac_mv(t, ps, tp):
            done["mv"] = A.put(lambda e: e.activation(mv[:, t, :], ps[:, :], ACT.Copy), tp)
            return [done["mv"]]

        gemm_a("mv", hT, evac_mv)
        t_moba = None
        gtok = {}
        for n in range(6):
            def evac(t, ps, tp, n=n):
                gtok[n, t] = A.put(lambda e: e.activation(gates[:, t, 512 * n:512 * n + 512], ps[:, :], ACT.Sigmoid), tp)
                return [gtok[n, t]]
            gemm_a(f"gt{n}", hT, evac)
            if t_moba is None and not any(q is t_gla for q in tasks):
                t_moba = spawn(moba())
        drain()
        if t_moba is None:
            t_moba = spawn(moba())
            drain()
        mt = {}

        def branch(i, xs, k0):
            sub = Split(xs.hi, xs.lo, xs.first + k0, 4)
            sub.tok = xs.tok[k0:k0 + 4]
            for n in range(2):
                def evac(t, ps, tp, n=n):
                    gsl = gates[:, t, 1024 * i + 512 * n:1024 * i + 512 * n + 512]
                    mx = mixed[:, t, 512 * n:512 * n + 512]
                    if i == 0:
                        mt[t, n] = V.put(lambda e: e.tensor_tensor(mx, ps[:, :], gsl, ALU.mult), tp,
                                         gtok[2 * i + n, t], *done["pool"])
                        return [mt[t, n]]
                    a = V.put(lambda e: e.tensor_tensor(mtmp[:, t, :], ps[:, :], gsl, ALU.mult), tp,
                              gtok[2 * i + n, t], *mt.get(("f", t), []))
                    mt[t, n] = V.put(lambda e: e.tensor_tensor(mx, mx, mtmp[:, t, :], ALU.add), a, mt[t, n])
                    mt["f", t] = [mt[t, n]]
                    return [a]
                gemm_a(f"br{i}{n}", sub, evac)

        branch(0, br, 0)
        to_split(brc, 0, 4, lambda t: yc[:, t, :], [done["yc"]])
        branch(1, br, 4)
        branch(2, brc, 0)
        to_split(br, 0, 8, lambda t: mixed[:, t, :], [mt[t, n] for t in range(2) for n in range(2)])
        A.wait(everything())
        x_tok = residual_rms("wo", br, fb1, t_row, t_x)

        def fin0(name, hid, fb):
            t_r = load(GD, "row2", row[:, :], bcast(io["norm_ffn_post"], D), *x_tok)
            return residual_rms(name, hid, fb, t_r, x_tok)

        x_tok = ffn("f0", "norm_ffn_pre", x_tok, fin0)

        x_tok = ffn("f1", "ffn1_norm_2", x_tok, lambda name, hid, fb: residual(name, hid, 0.5, x_tok))

        m2 = Phase("m2")
        w1_off = m2.off
        Pb2 = m2.new("Pb", [128, 8, T])
        PT2 = m2.new("PT", [128, 16, 128])
        y2 = m2.new("y", [128, 2, D])
        ytmp = m2.new("ytmp", [128, 2, 512])
        m2.new("pad", [128, 1024])
        w1 = [m2.new(f"w1{i}", [128, 16, 256], off=w1_off + 16384 * i) for i in range(2)]
        u_hi, u_lo = m2.new("u_hi", [128, 8, T], F32R), m2.new("u_lo", [128, 8, T], F32R)
        gg_off = m2.off
        gg = m2.new("gg", [128, 2, 2048])
        xn2 = m2.new("xn", [128, 2, D], off=gg_off)
        qn = m2.new("qn", [128, 4, T])
        ksw = m2.new("ksw", [128, 2, T])
        vsw = m2.new("vsw", [128, 2, 256])
        qf, kf = m2.new("qf", [128, 4, T]), m2.new("kf", [128, 4, T])
        vf = m2.new("vf", [128, 2, 512])
        rel = m2.new("rel", [128, 8 * 384])
        R = [m2.new(f"R{i}", [128, 16, 2, 15]) for i in range(2)]
        w2k = m2.new("w2k", [128, 2, 128])
        w2v = m2.new("w2v", [128, 2, 64])
        gel = [m2.new(f"gel{i}", [128, 2, 30]) for i in range(2)]
        ps_nat = m2.new("pos", [128, 2, 128])
        posT = m2.new("posT", [128, 2, 16])
        kcT = m2.new("kcT", [128, 32])
        vc = m2.new("vc", [128, 2, 64])
        gf = m2.new("gf", [128, 2, 32])
        onsa, ofox = m2.new("onsa", [128, 2, 512]), m2.new("ofox", [128, 2, 512])
        hot = m2.new("hot", [128, 512])
        tbl = m2.new("tbl", [128, 8])
        Xr = m2.new("Xr", [128, 512], off=m2.off - 0)
        m2.off += 2048
        sel = m2.new("sel", [128, 8, 128])
        fx = m2.new("fx", [128, 3, 256])
        Pc = m2.new("Pc", [128, 8, 16])
        PcT = m2.new("PcT", [128, 8, 128], off=w1_off + 24576)
        otmp = m2.new("otmp", [128, 8, 64])
        scr = nc.dram_tensor("scratch", [8, 512], F32).ap()
        wide = nc.dram_tensor("wide", [128, 4096], F32).ap()

        here = everything()
        for q in (A, V):
            q.wait(here)
        norm_t(x, xn2, x_tok, "mix_norm_2", hT)
        lw = [load(GD, f"w1{i}", w1[i][:, :, :], io[n].rearrange("a (i p) h -> p (a i) h", p=128), *here)
              for i, n in enumerate(("cmp_k_w1_2", "cmp_v_w1_2"))]
        lp = [load(GD, f"pos{i}", ps_nat[0:16, i, :], io[n].rearrange("a (i r) d -> (a i) (r d)", r=2))
              for i, n in enumerate(("cmp_pos_k_2", "cmp_pos_v_2"))]
        l2 = [load(GD, f"w2k{i}", w2k[:, :, 64 * i:64 * i + 64], io["cmp_k_w2_2"].rearrange("a (k p) d -> p (a k) d", p=128))
              for i in range(2)]
        l2.append(load(GD, "w2v", w2v[:, :, :], io["cmp_v_w2_2"].rearrange("a (k p) d -> p (a k) d", p=128)))
        t_hot = load(GD, "hot", hot[0:33, :], io["c_hot"])
        tz = V.put(lambda e: e.memset(tbl[32:33, :], NEG))
        t_tbl = load(GD, "tbl", tbl[0:32, :], io["rel_bias_table_2"])
        t_sel = load(GD, "sel", sel[0:8, :, :], io["c_sel"].rearrange("k (h i) -> k h i", h=8))

        def rel_bias():
            s = SR.get()
            s0 = s
            tp = P.put(lambda e: e.matmul(s0.ap[0:8, :], tbl[0:33, :], hot[0:33, :], start=True, stop=True),
                       t_hot, t_tbl, tz, *s0.free)
            tv = V.put(lambda e: e.tensor_copy(Xr[0:8, :], s0.ap[0:8, :]), tp)
            s0.free = [tv]
            td = load(GD, "scr", scr, Xr[0:8, :], tv)
            td = load(GD, "wide", wide, bcast(scr, 4096), td)
            done["rel"] = []
            for qb in range(2):
                L = 128 * (qb + 1)
                src = bass.AP(tensor=wide.tensor, offset=255 - 128 * qb, ap=[[4095, 128], [512, 8], [1, L]])
                dst = rel[:, (0, 1024)[qb]:(1024, 3072)[qb]].rearrange("p (h k) -> p h k", h=8)
                done["rel"].append(load(GD, f"rel{qb}", dst, src, td))
            s = SR.get()

            def tr(e):
                for i in range(2):
                    r = e.transpose(s.ap[:, 16 * i:16 * i + 16], ps_nat[0:16, i, :], ident[0:16, 0:16])
                return r

            tp = P.put(tr, *lp, *s.free)
            done["posT"] = V.put(lambda e: e.tensor_copy(posT[:, :, :], s.ap[:, 0:32].rearrange("p (i r) -> p i r", i=2)), tp)
            s.free = [done["posT"]]

        rel_bias()

        def evac_kv(i, ps, tp):
            for g in range(2):
                for half in range(2):
                    pa = slice(64 * half, 64 * half + 64)
                    src = ps[pa, 256 * g + half:256 * g + 256:2].rearrange("p (c j) -> p j c", j=8)
                    for top_half in range(2):
                        sv = src[:, :, top_half:top_half + 15]
                        o = R[i][pa, 8 * top_half:8 * top_half + 8, g, :]
                        pt = posT[pa, i, 8 * top_half:8 * top_half + 8].unsqueeze(2).to_broadcast([64, 8, 15])
                        t = V.put(lambda e, o=o, sv=sv, pt=pt: e.tensor_tensor(o, sv, pt, ALU.add), tp, done["posT"])
            done["R", i] = t
            return [t]

        def bound_rel(qb, h):
            o, L = (0, 128) if qb == 0 else (1024, 256)
            return rel[:, o + L * h:o + L * h + L]

        def tile_of(h):
            return slice(64 * (h // 4), 64 * (h // 4) + 64), h % 4

        def nsa():
            for i in range(2):
                s = SR.get()

                def c1(e, s=s, i=i):
                    for f in range(2):
                        for j in range(16):
                            r = e.matmul(s.ap[:, 32 * f:32 * f + 30], w1[i][:, j, 128 * f:128 * f + 128],
                                         R[i][:, j, :, :].rearrange("p g c -> p (g c)"), start=j == 0, stop=j == 15)
                    return r

                tp = P.put(c1, done["R", i], lw[i], *s.free)
                ta = A.put(lambda e, s=s, i=i: e.activation(
                    gel[i][:, :, :], s.ap[:, 0:64].rearrange("p (f c) -> p f c", f=2)[:, :, 0:30],
                    ACT.Gelu_apprx_tanh), tp)
                s.free = [ta]
                yield
            s = SR.get()

            def c2(e, s=s):
                for f in range(2):
                    r = e.matmul(s.ap[:, 0:30], w2k[:, f, :], gel[0][:, f, :], start=f == 0, stop=f == 1)
                for g in range(2):
                    for f in range(2):
                        r = e.matmul(s.ap[0:15, 64 + 64 * g:128 + 64 * g], gel[1][:, f, 15 * g:15 * g + 15], w2v[:, f, :],
                                     start=f == 0, stop=f == 1)
                return r

            tp = P.put(c2, ta, *l2, *s.free)
            for g in range(2):
                pa = slice(64 * g, 64 * g + 64)
                V.put(lambda e, pa=pa, g=g, s=s: e.tensor_copy(kcT[pa, 0:15], s.ap[pa, 15 * g:15 * g + 15]), tp)
            tk = V.put(lambda e, s=s: e.tensor_copy(vc[0:15, :, :], s.ap[0:15, 64:192].rearrange("p (g d) -> p g d", g=2)), tp)
            s.free = [tk]
            yield
            tco = None
            for qb in range(2):
                n = (7, 15)[qb]
                o_rel, L = (0, 128) if qb == 0 else (1024, 256)
                mx, sums, rec = small(8), small(8), small(8)
                tps = []
                ss = [SR.get(), SR.get()]

                def sc(e, ss=ss, qb=qb, n=n):
                    for h in range(8):
                        pa, ti = tile_of(h)
                        r = e.matmul(ss[h // 4].ap[:, 16 * ti:16 * ti + n], qn[pa, ti, 128 * qb:128 * qb + 128],
                                     kcT[pa, 0:n], start=True, stop=True)
                    return r

                tp = P.put(sc, tk, done["qn"], *ss[0].free, *ss[1].free)
                for h in range(8):
                    bsl = bound_rel(qb, h)[:, 31:31 + 16 * (n - 1) + 1:16]
                    tv = V.put(lambda e, h=h, n=n, bsl=bsl, mx=mx, ss=ss: e.tensor_tensor_reduce(
                        Pc[:, h, 0:n], ss[h // 4].ap[:, 16 * (h % 4):16 * (h % 4) + n], bsl, 1.0, -3.0e38,
                        ALU.add, ALU.max, mx[:, h:h + 1]), tp, *done["rel"], *([tco] if tco else []))
                ss[0].free = ss[1].free = [tv]
                te = softmax_block(Pc, mx, sums, 8, n, [tv])
                tr = V.put(lambda e, rec=rec, sums=sums: e.reciprocal(rec, sums), te)
                co = small(8)
                tr = V.put(lambda e, co=co, rec=rec, qb=qb: e.tensor_tensor(co, rec, gf[:, qb, 0:8], ALU.mult), tr, done["gf"])
                if qb == 0:
                    tr = V.put(lambda e, co=co: e.tensor_scalar(co, co, cst[:, C_ROW:C_ROW + 1], None, ALU.mult), tr)
                yield
                sl = [SR.get(), SR.get()]

                def tr8(e, sl=sl, n=n):
                    for h in range(8):
                        r = e.transpose(sl[h // 4].ap[0:n, 128 * (h % 4):128 * (h % 4) + 128], Pc[:, h, 0:n], ident)
                    return r

                tp = P.put(tr8, te, *sl[0].free, *sl[1].free)
                for i in range(2):
                    tc = V.put(lambda e, i=i, sl=sl, n=n: e.tensor_copy(
                        PcT[0:n, 4 * i:4 * i + 4, :], sl[i].ap[0:n, :].rearrange("p (h t) -> p h t", h=4)), tp, done["w1_read"])
                    sl[i].free = [tc]
                tco = tp
                yield
                s = SR.get()

                def pv(e, s=s, n=n):
                    for h in range(8):
                        r = e.matmul(s.ap[:, 64 * h:64 * h + 64], PcT[0:n, h, :], vc[0:n, h // 4, :], start=True, stop=True)
                    return r

                tp = P.put(pv, tc, tk, *s.free)
                o = onsa[:, qb, :].rearrange("p (h d) -> p h d", h=8)
                done["onsa", qb] = V.put(lambda e, o=o, s=s, co=co: e.tensor_tensor(
                    o, s.ap[:, :].rearrange("p (h d) -> p h d", h=8), spread(co, 64), ALU.mult), tp, tr)
                s.free = [done["onsa", qb]]
                yield
            for w in range(2):
                def score(e, ps, h, qb, L, w=w):
                    pa, ti = tile_of(h)
                    return e.matmul(ps, qn[pa, ti, 128 * qb:128 * qb + 128], ksw[pa, w, 0:L], start=True, stop=True)

                def out(qb, ps, rec, after, w=w):
                    co = small(8)
                    o = onsa[:, qb, :].rearrange("p (h d) -> p h d", h=8)
                    t = V.put(lambda e: e.tensor_tensor(co, rec, gf[:, qb, 8 + 8 * w:16 + 8 * w], ALU.mult), *after, done["gf"])
                    a = V.put(lambda e: e.tensor_tensor(otmp[:, :, :], ps, spread(co, 64), ALU.mult), t)
                    done["onsa", qb] = V.put(lambda e: e.tensor_tensor(o, o, otmp[:, :, :], ALU.add), a, done["onsa", qb])
                    return [a]

                yield from attention(Pb2, PT2, score, bound_rel,
                                      lambda h, k, w=w: vsw[:, k, 128 * w + 64 * (h // 4):128 * w + 64 * (h // 4) + 64],
                                      [done["qn"], done["ksw"], *done["rel"]], [done["vsw"]], out, [P.last], range(8))
            to_split(us, 0, 4, lambda t: onsa[:, t, :], [done["onsa", 0], done["onsa", 1]])

        us = Split(u_hi, u_lo, 0, 8)
        yT = Split(hT_hi, hT_lo, 0, 8)

        def fox():
            s = SR.get()

            def tr(e):
                for t in range(2):
                    r = e.transpose(s.ap[0:8, 128 * t:128 * t + 128], gf[:, t, 24:32], ident)
                return r

            tp = P.put(tr, done["gf_raw"], *s.free)
            bf = cols[0:8, COLS["mix_b_forget_2"][0]:COLS["mix_b_forget_2"][0] + 1]
            z = s.ap[0:8, 0:256]
            ta = A.put(lambda e: e.activation(fx[0:8, 0, :], z, ACT.Abs, bias=bf), tp, t_cols)
            tv = V.put(lambda e: e.tensor_scalar(fx[0:8, 1, :], z, bf, 0.0, ALU.add, ALU.min), ta, t_cols)
            s.free = [ta, tv]
            ta = A.put(lambda e: e.activation(fx[0:8, 0, :], fx[0:8, 0, :], ACT.Exp, scale=-1.0), ta)
            ta = A.put(lambda e: e.activation(fx[0:8, 0, :], fx[0:8, 0, :], ACT.Ln, bias=1.0), ta)
            tv = V.put(lambda e: e.tensor_tensor(fx[0:8, 1, :], fx[0:8, 1, :], fx[0:8, 0, :], ALU.subtract), ta, tv)
            to = V.put(lambda e: e.memset(fx[0:8, 0, :], 1.0), tv)
            tc = V.put(lambda e: e.tensor_tensor_scan(fx[0:8, 2, :], fx[0:8, 0, :], fx[0:8, 1, :], 0.0,
                                                      ALU.mult, ALU.add), tv, to)
            yield

            def score(e, ps, h, qb, L):
                pa = slice(64 * (h % 2), 64 * (h % 2) + 64)
                e.matmul(ps, qf[pa, h // 2, 128 * qb:128 * qb + 128], kf[pa, h // 2, 0:L], start=True, stop=False)
                return e.matmul(ps, sel[0:8, h, :], fx[0:8, 2, 0:L], start=False, stop=True)

            def bias(qb, h):
                o, L = (0, 128) if qb == 0 else (128, 256)
                return cst[:, C_CM + o:C_CM + o + L]

            def out(qb, ps, rec, after):
                o = ofox[:, qb, :].rearrange("p (h d) -> p h d", h=8)
                done["ofox"] = V.put(lambda e: e.tensor_tensor(o, ps, spread(rec, 64), ALU.mult), *after)
                return [done["ofox"]]

            yield from attention(Pb2, PT2, score, bias, lambda h, k: vf[:, k, 64 * h:64 * h + 64],
                                 [done["qf"], done["kf"], tc, t_sel], [done["vf"]], out, [P.last])
            to_split(us, 4, 4, lambda t: ofox[:, t, :], [done["ofox"]])

        gemm_b("kv", hT, evac_kv)

        def evac_gf(t, ps, tp):
            a = A.put(lambda e: e.activation(gf[:, t, 0:24], ps[:, 0:24], ACT.Sigmoid), tp)
            done["gf"] = done["gf_raw"] = A.put(lambda e: e.activation(gf[:, t, 24:32], ps[:, 24:32], ACT.Copy), tp)
            return [done["gf"]]

        gemm_a("gf", hT, evac_gf)
        gemm_b("qn", hT, keep_b("qn", qn, 0.125))

        def evac_ksw(i, ps, tp):
            p2 = ps[:, :].rearrange("p (i t) -> p i t", i=2)
            done["ksw"] = A.put(lambda e: e.activation(ksw[:, :, :], p2, ACT.Copy), tp)
            return [done["ksw"]]

        gemm_b("ksw", hT, evac_ksw)

        def evac_tm(key, out):
            def evac(t, ps, tp):
                o = out[:, t, :]
                done[key] = A.put(lambda e: e.activation(o, ps[:, 0:o.shape[-1]], ACT.Copy), tp)
                return [done[key]]
            return evac

        gemm_a("vsw", hT, evac_tm("vsw", vsw))

        def both():
            g = nsa()
            yield from g
            yield from fox()

        done["w1_read"] = P.last
        spawn(both())
        gemm_b("qf", hT, keep_b("qf", qf, 0.125))
        gemm_b("kf", hT, keep_b("kf", kf))
        gemm_a("vf", hT, evac_tm("vf", vf))
        ggt = {}
        for n in range(4):
            def evac(t, ps, tp, n=n):
                ggt[n, t] = A.put(lambda e: e.activation(gg[:, t, 512 * n:512 * n + 512], ps[:, :], ACT.Sigmoid), tp)
                return [ggt[n, t]]
            gemm_a(f"gg{n}", hT, evac)
        drain()
        yt = {}
        for i in range(2):
            sub = Split(u_hi, u_lo, 4 * i, 4)
            sub.tok = us.tok[4 * i:4 * i + 4]
            for n in range(2):
                def evac(t, ps, tp, n=n, i=i):
                    gsl = gg[:, t, 1024 * i + 512 * n:1024 * i + 512 * n + 512]
                    yy = y2[:, t, 512 * n:512 * n + 512]
                    if i == 0:
                        yt[t, n] = V.put(lambda e: e.tensor_tensor(yy, ps[:, :], gsl, ALU.mult), tp, ggt[2 * i + n, t])
                        return [yt[t, n]]
                    a = V.put(lambda e: e.tensor_tensor(ytmp[:, t, :], ps[:, :], gsl, ALU.mult), tp, ggt[2 * i + n, t],
                              *yt.get(("f", t), []))
                    yt[t, n] = V.put(lambda e: e.tensor_tensor(yy, yy, ytmp[:, t, :], ALU.add), a, yt[t, n])
                    yt["f", t] = [yt[t, n]]
                    return [a]
                gemm_a(f"up{i}{n}", sub, evac)
        to_split(yT, 0, 8, lambda t: y2[:, t, :], [yt[t, n] for t in range(2) for n in range(2)])

        cm = Phase("cm")
        mT_hi, mT_lo = cm.new("mT_hi", [128, 8, T], F32R), cm.new("mT_lo", [128, 8, T], F32R)
        memx = cm.new("memx", [128, 2, D])
        xnm = cm.new("xnm", [128, 2, D])
        xnc = cm.new("xnc", [128, 2, D])
        ckT = cm.new("ckT", [128, 8, T])
        cv = cm.new("cv", [128, 2, D])
        cqT = cm.new("cqT", [128, 8, T])
        cP = cm.new("cP", [128, 4, T])
        cPT = cm.new("cPT", [128, 8, 128])
        co = cm.new("co", [128, 2, D])
        mT = Split(mT_hi, mT_lo, 0, 8)
        oT = Split(mT_hi, mT_lo, 0, 8)
        here = everything()
        t_mem = load(GD, "mem", memx[:, :, :], io["mem_2"].rearrange("a (k p) d -> p (a k) d", p=128), *here)
        x_tok = residual("mo", yT, 1.0, x_tok)
        for q in (A, V):
            q.wait(here)
        norm_t(memx, xnm, [t_mem, t_mem], "mem_kv_norm_2", mT)

        def early_q():
            yield
            norm_t(x, xnc, x_tok, "mem_q_norm_2", hT)

        spawn(early_q())
        for n in range(2):
            gemm_b(f"mkv{n}", mT, keep_b("ckT", ckT[:, 4 * n:4 * n + 4, :]))
        for n in range(2):
            def evac(t, ps, tp, n=n):
                done["cv"] = A.put(lambda e: e.activation(cv[:, t, 512 * n:512 * n + 512], ps[:, :], ACT.Copy), tp)
                return [done["cv"]]
            gemm_a(f"mkv{2 + n}", mT, evac)
        drain()
        for n in range(2):
            gemm_b(f"cq{n}", hT, keep_b("cqT", cqT[:, 4 * n:4 * n + 4, :], 1.0 / 16))
        p_free = []
        for qb in range(2):
            mx, sums, rec, nm = small(4), small(4), small(4), small(4)
            for g in range(2):
                s = SR.get()

                def sc(e, s=s, g=g, qb=qb):
                    for i in range(2):
                        for k in range(2):
                            f = 2 * (2 * g + i) + k
                            r = e.matmul(s.ap[:, 256 * i:256 * i + 256], cqT[:, f, 128 * qb:128 * qb + 128], ckT[:, f, :],
                                         start=k == 0, stop=k == 1)
                    return r

                tp = P.put(sc, done["cqT"], done["ckT"], *s.free)
                p2 = s.ap[:, :].rearrange("p (i t) -> p i t", i=2)
                tv = V.put(lambda e, p2=p2, g=g, mx=mx: e.tensor_reduce(mx[:, 2 * g:2 * g + 2], p2, AX, ALU.max), tp)
                tv = V.put(lambda e, g=g, mx=mx, nm=nm: e.tensor_scalar(nm[:, 2 * g:2 * g + 2], mx[:, 2 * g:2 * g + 2], -1.0, None,
                                                                       ALU.mult), tv)
                for i in range(2):
                    h = 2 * g + i
                    te = A.put(lambda e, p2=p2, i=i, h=h, nm=nm, sums=sums: e.activation(
                        cP[:, h, :], p2[:, i, :], ACT.Exp, bias=nm[:, h:h + 1], accum_out=sums[:, h:h + 1]), tv, *p_free)
                s.free = [te]
            tr = V.put(lambda e, rec=rec, sums=sums: e.reciprocal(rec, sums), te)
            for b in range(2):
                s = SR.get()

                def tr4(e, s=s, b=b):
                    for i in range(4):
                        h, k = 2 * b + i // 2, i % 2
                        r = e.transpose(s.ap[:, 128 * i:128 * i + 128], cP[:, h, 128 * k:128 * k + 128], ident)
                    return r

                tp = P.put(tr4, te, *s.free)
                tc = V.put(lambda e, s=s, b=b: e.tensor_copy(
                    cPT[:, 4 * b:4 * b + 4, :], s.ap[:, :].rearrange("p (i t) -> p i t", i=4)), tp)
                s.free = [tc]
            p_free = [tp]
            for g in range(2):
                s = SR.get()

                def pv(e, s=s, g=g):
                    for i in range(2):
                        h = 2 * g + i
                        for k in range(2):
                            r = e.matmul(s.ap[:, 256 * i:256 * i + 256], cPT[:, 2 * h + k, :], cv[:, k, 256 * h:256 * h + 256],
                                         start=k == 0, stop=k == 1)
                    return r

                tp = P.put(pv, tc, done["cv"], *s.free)
                for i in range(2):
                    h = 2 * g + i
                    tv = V.put(lambda e, s=s, i=i, h=h, qb=qb, rec=rec: e.tensor_scalar(
                        co[:, qb, 256 * h:256 * h + 256], s.ap[:, 256 * i:256 * i + 256], rec[:, h:h + 1], None, ALU.mult), tp, tr)
                s.free = [tv]
        to_split(oT, 0, 8, lambda t: co[:, t, :], [tv])
        x_tok = residual("co", oT, 1.0, x_tok)

        t_row3 = load(GD, "row3", row[:, :], bcast(io["final_norm_2"], D), *everything())
        x_tok = ffn("f2", "ffn2_norm_2", x_tok, lambda name, hid, fb: residual(name, hid, 0.5, x_tok))
        ph = Phase("end")
        xe = ph.new("xe", [128, 2, D])
        A.wait(everything())
        tt = rms_scaled(x, xe, x_tok)
        oo = io["out"].rearrange("a (k p) d -> p (a k) d", p=128)
        for t in range(2):
            tv = V.put(lambda e, t=t: e.tensor_tensor(xe[:, t, :], xe[:, t, :], row[:, :], ALU.mult), tt[t], t_row3)
            t_out = SP.put(s_out, cnt, oo[:, t, :], xe[:, t, :], tv)
        assert nxt[0] == len(units)

        block = ctx.enter_context(nc.Block())

        @block.sync
        def _(eng):
            SP.run(eng)
            eng.wait_ge(s_out, t_out[1])

        @block.scalar
        def _(eng):
            AD.run(eng)
            A.run(eng)

        @block.vector
        def _(eng):
            V.run(eng)

        @block.tensor
        def _(eng):
            P.run(eng)

        @block.gpsimd
        def _(eng):
            GD.run(eng)


_RAW = ["x", "gla_w_g2", "pool_w", "gla_norm", "norm_mix_post", "norm_ffn_post", "mem_2", "rel_bias_table_2",
        "cmp_pos_k_2", "cmp_pos_v_2", "cmp_k_w1_2", "cmp_k_w2_2", "cmp_v_w1_2", "cmp_v_w2_2", "final_norm_2"]


def lay_out(inputs):
    arrays = {n: np.ascontiguousarray(inputs[n]) for n in _RAW}
    units, chunks, total = unit_plan()
    flat = np.empty(total, np.float32)
    for name, weight, cols, rows in weight_chunks():
        ws = weight if isinstance(weight, tuple) else (weight,)
        w = np.concatenate([np.asarray(inputs[n])[0][:, cols] for n in ws], 1)
        for u in chunks[name]:
            off, k, n, k0 = units[u]
            part = w[128 * k0:128 * (k0 + k)].reshape(k, 128, n).transpose(1, 0, 2)
            flat[off:off + 128 * k * n] = part.reshape(-1)
    arrays["wflat"] = flat
    cols = np.zeros((128, N_COLS), np.float32)
    for name, (c, w) in COLS.items():
        v = np.asarray(inputs[name]).reshape(-1)
        if len(v) == 8:
            cols[0:8, c] = v
        else:
            cols[:, c:c + w] = v.reshape(w, 128).T
    arrays["cols"] = cols
    arrays.update(constants())
    return arrays


def kernel(**inputs):
    import concourse.bacc as bacc
    from concourse.bass_utils import run_bass_kernel_spmd

    nc = bacc.Bacc("TRN2", target_bir_lowering=False, num_devices=1)
    arrays = {f"in_{n}": a for n, a in lay_out(inputs).items()}
    io = {n[3:]: nc.dram_tensor(n, a.shape, mybir.dt.from_np(a.dtype), kind="ExternalInput").ap()
          for n, a in arrays.items()}
    io["out"] = nc.dram_tensor("out", (1, T, D), F32, kind="ExternalOutput").ap()
    build(nc, io)
    r = run_bass_kernel_spmd(nc, [arrays], core_ids=[0])
    return r.results[0]["out"]
```

```python
from contextlib import ExitStack

import numpy as np

import concourse.bass as bass
from concourse import mybir

F32 = mybir.dt.float32
F32R = mybir.dt.float32r
U8 = mybir.dt.uint8
ALU = mybir.AluOpType
ACT = mybir.ActivationFunctionType
AX = mybir.AxisListType.X

NEG = -1e30
EPS = 1e-6
T = 256
D = 1024
FF = 2816
UNIT = 1024
NRAW = 4
NSPL = 4
AHEAD = 2
START, ROOM = 16512, 212832


def _cols(*spans):
    return np.concatenate([np.arange(a, b) for a, b in spans])


def weight_chunks():
    out = []

    def add(name, weight, cols, rows):
        out.append((name, weight, cols, rows))

    def halves(name, weight, rows):
        for n in range(2):
            add(f"{name}{n}", weight, _cols((512 * n, 512 * n + 512)), rows)

    def ffn(name, gate, up, down):
        for c in range(11):
            add(f"{name}gu{c}", (gate, up), _cols((256 * c, 256 * c + 256)), D)
        halves(f"{name}dn", down, FF)

    for name, a, b in (("qk", 0, 512), ("g1", 1024, 1040), ("gv", 512, 1024), ("gr", 1040, 1552),
                       ("pu", 1552, 2064), ("mq", 2064, 2576), ("mk", 2576, 3088), ("mv", 3088, 3600)):
        add(name, "w_in", _cols((a, b)), D)
    for n in range(6):
        add(f"gt{n}", "w_in", _cols((3600 + 512 * n, 4112 + 512 * n)), D)
    halves("br0", "w_branch_a", 512)
    halves("br1", "w_branch_b", 512)
    halves("br2", "w_branch_c", 512)
    halves("wo", "w_out", D)
    ffn("f0", "ffn_w_gate", "ffn_w_up", "ffn_w_down")
    ffn("f1", "ffn1_w_gate_2", "ffn1_w_up_2", "ffn1_w_down_2")
    w = "mix_w_in_2"
    add("qf", w, _cols((1304, 1816)), D)
    add("kf", w, _cols((1816, 2328)), D)
    add("vf", w, _cols((2328, 2840)), D)
    add("gf", w, _cols((2840, 2848), (1280, 1304)), D)
    add("kv", w, _cols((512, 576), (512, 576), (576, 640), (576, 640),
                       (640, 704), (640, 704), (704, 768), (704, 768)), D)
    add("qn", w, _cols(*[(64 * (4 * g + i), 64 * (4 * g + i) + 64) for i in range(4) for g in range(2)]), D)
    add("ksw", w, _cols((768, 896), (1024, 1152)), D)
    add("vsw", w, _cols((896, 1024), (1152, 1280)), D)
    for n in range(4):
        add(f"gg{n}", w, _cols((2848 + 512 * n, 3360 + 512 * n)), D)
    for n in range(4):
        add(f"mkv{n}", "mem_w_kv_2", _cols((512 * n, 512 * n + 512)), D)
    halves("up1", "w_up_fox_2", 512)
    halves("up0", "w_up_nsa_2", 512)
    halves("mo", "mix_w_out_2", D)
    halves("cq", "mem_w_q_2", D)
    halves("co", "mem_w_o_2", D)
    ffn("f2", "ffn2_w_gate_2", "ffn2_w_up_2", "ffn2_w_down_2")
    return out


def unit_plan():
    units, chunks, at = [], {}, 0
    for name, weight, cols, rows in weight_chunks():
        n = len(cols) * (2 if isinstance(weight, tuple) else 1)
        kt = min(rows // 128, max(1, UNIT // n))
        ids = []
        for k0 in range(0, rows // 128, kt):
            k = min(kt, rows // 128 - k0)
            ids.append(len(units))
            units.append((at, k, n, k0))
            at += 128 * k * n
        chunks[name] = ids
    return units, chunks, at


MASKS = [1, 2, 4, 8, 16, 32, 64]
C_ID, C_CM, C_INV, C_ROW, C_RST = 0, 128, 512, 576, 577
C_ALL = 577 + 256


def constants():
    f = np.float32
    c = np.zeros((128, C_ALL), f)
    c[:, C_ID:C_ID + 128] = np.eye(128, dtype=f)
    q = np.arange(128)[:, None]
    c[:, C_CM:C_CM + 128] = np.where(np.arange(128)[None] <= q, 0, NEG)
    c[:, C_CM + 128:C_CM + 384] = np.where(np.arange(256)[None] <= q + 128, 0, NEG)
    for g in range(4):
        c[:, C_INV + 16 * g:C_INV + 16 * g + 16] = 1.0 / np.minimum(np.arange(16) + 1, 2 << g).astype(f)
    c[:, C_ROW] = (np.arange(128) >= 31)
    c[:, C_RST:C_RST + 256] = (np.arange(256) % 64 != 0)
    t = np.arange(128)
    s = t[:, None]
    masks = [(s // (2 * m) == t // (2 * m)) & (s % (2 * m) < m) & (t % (2 * m) >= m) for m in MASKS]
    masks = np.stack(masks + [s == t], 1).astype(f).reshape(128, 8 * 128)
    slope = (2.0 ** (-8.0 * (np.arange(8) + 1) / 8)).astype(f)
    parts = []
    for qb in range(2):
        tq = np.arange(128)[:, None, None] + 128 * qb
        k = np.arange(128 * (qb + 1))[None, None]
        b = -(slope[None, :, None] * (tq - k).astype(f))
        parts.append(np.where(k <= tq, b, NEG).astype(f).reshape(128, -1))
    alibi = np.concatenate(parts, 1)
    hot = np.zeros((33, 512), f)
    dist = 255 - np.arange(512)
    n = np.maximum(dist, 0)
    large = 16 + (np.log(np.maximum(n, 1).astype(f) / f(16)) / f(np.log(8.0)) * f(16)).astype(np.int32)
    bucket = np.where(n < 16, n, np.minimum(large, 31))
    for u in range(512):
        hot[bucket[u] if dist[u] >= 0 else 32, u] = 1
    sel = np.zeros((8, 8, 128), f)
    for h in range(8):
        sel[h, h] = -1
    return {"c_cst": c, "c_masks": masks, "c_alibi": alibi, "c_hot": hot, "c_sel": sel.reshape(8, 1024)}


COLS = {}
for _n, _w in (("norm_mix_pre", 8), ("norm_ffn_pre", 8), ("pool_scale", 4), ("gla_b_g", 2), ("ffn1_norm_2", 8),
               ("mix_norm_2", 8), ("mem_q_norm_2", 8), ("mem_kv_norm_2", 8), ("ffn2_norm_2", 8), ("mix_b_forget_2", 1)):
    COLS[_n] = (sum(w for _, w in COLS.values()), _w)
N_COLS = sum(w for _, w in COLS.values())


class Queue:

    def __init__(self, sem):
        self.sem, self.n, self.seen, self.items = sem, 0, {}, []

    def wait(self, after):
        for sem, v in after:
            if self.seen.get(sem.name, 0) < v:
                self.seen[sem.name] = v
                self.items.append((sem, v))

    def put(self, fn, *after):
        self.wait(after)
        self.n += 1
        self.items.append((fn, None))
        return self.last

    @property
    def last(self):
        return (self.sem, self.n)

    def run(self, eng):
        for a, v in self.items:
            if v is not None:
                eng.wait_ge(a, v)
            else:
                a(eng).then_inc(self.sem, 1)


class DmaQueue:

    def __init__(self):
        self.items, self.seen = [], {}

    def put(self, sem, count, out, in_, *after):
        for s, v in after:
            if self.seen.get(s.name, 0) < v:
                self.seen[s.name] = v
                self.items.append((s, v, None, None))
        count[sem.name] = count.get(sem.name, 0) + 16
        self.items.append((sem, None, out, in_))
        return (sem, count[sem.name])

    def run(self, eng):
        for s, v, out, in_ in self.items:
            if v is not None:
                eng.wait_ge(s, v)
            else:
                eng.dma_start(out, in_).then_inc(s, 16)


class Slot:
    def __init__(self, ap):
        self.ap, self.free = ap, []


class Ring:
    def __init__(self, aps):
        self.slots, self.i = [Slot(a) for a in aps], 0

    def get(self):
        self.i += 1
        return self.slots[(self.i - 1) % len(self.slots)]


class Split:

    def __init__(self, hi, lo, first, n):
        self.hi, self.lo, self.first, self.tok = hi, lo, first, [None] * n

    def h(self, k):
        return self.hi[:, self.first + k, :]

    def l(self, k):
        return self.lo[:, self.first + k, :]


def build(nc, io):
    with ExitStack() as ctx:
        def sem(name):
            return ctx.enter_context(nc.semaphore(name))

        P, A, V = Queue(sem("s_pe")), Queue(sem("s_act")), Queue(sem("s_dve"))
        G = Queue(sem("s_pool"))
        SP, AD = DmaQueue(), DmaQueue()
        cnt = {}
        S_RAW = [sem(f"s_raw{i}") for i in range(NRAW)]
        s_out = sem("s_out")

        ctx.enter_context(nc.sbuf_tensor("slab", [128, ROOM // 4], F32))
        top = [START]

        def at(name, shape, dt, off):
            return nc.alloc_sbuf_tensor_at(name, shape, dt, offset=off)

        def fixed(name, shape, dt=F32):
            size = int(np.prod(shape[1:])) * (1 if dt == U8 else 4)
            t = at(name, shape, dt, top[0])
            top[0] += (size + 31) // 32 * 32
            return t

        raw = [fixed(f"raw{i}", [128, UNIT]) for i in range(NRAW)]
        whi = [fixed(f"whi{i}", [128, UNIT], F32R) for i in range(NSPL)]
        wlo = [fixed(f"wlo{i}", [128, UNIT], F32R) for i in range(NSPL)]
        x = fixed("x", [128, 2, D])
        hT_hi = fixed("hT_hi", [128, 8, T], F32R)
        hT_lo = fixed("hT_lo", [128, 8, T], F32R)
        cst = fixed("cst", [128, C_ALL])
        cols = fixed("cols", [128, N_COLS])
        row = fixed("row", [128, D])
        sm = fixed("sm", [128, 384])
        stat = fixed("stat", [128, 64])
        junk = fixed("junk", [128, 512])
        expo = fixed("expo", [128, 8])
        ones = fixed("ones", [128, 128])
        diag = fixed("diag", [128, 2, 128])
        rTs = [fixed(f"rT{i}", [128, T]) for i in range(2)]
        arena = top[0]
        m2_late = arena + 61440
        limit = START + ROOM
        ident = cst[:, C_ID:C_ID + 128]

        class Phase:

            def __init__(self, tag):
                self.tag, self.off = tag, arena

            def new(self, name, shape, dt=F32, off=None):
                size = (int(np.prod(shape[1:])) * (1 if dt == U8 else 4) + 31) // 32 * 32
                o = self.off if off is None else off
                t = at(f"{self.tag}_{name}", shape, dt, o)
                if off is None:
                    self.off += size
                assert max(self.off, o + size) <= limit, (name, self.off - limit)
                return t

        sm_at = [0]

        def small(n):
            if sm_at[0] + n > 384:
                sm_at[0] = 0
            sm_at[0] += n
            return sm[:, sm_at[0] - n:sm_at[0]]

        banks = [ctx.enter_context(nc.psum_tensor(f"ps{i}", [128, 512], F32)) for i in range(8)]
        GR, SR = Ring(banks[0:4]), Ring(banks[4:8])

        def load(q, name, out, in_, *after):
            return q.put(sem("l_" + name), cnt, out, in_, *after)

        def bcast(ap, n):
            return bass.AP(tensor=ap.tensor, offset=ap.offset, ap=[[0, 128], [1, n]])

        xin = io["x"].rearrange("a (k p) d -> p (a k) d", p=128)
        t_x = [load(SP, f"x{t}", x[:, t, :], xin[:, t, :]) for t in range(2)]
        t_cst = load(AD, "ident", cst[:, 0:128], io["c_cst"][:, 0:128])
        t_rest = load(AD, "cst", cst[:, 128:C_ALL], io["c_cst"][:, 128:C_ALL])
        t_cols = load(AD, "cols", cols[:, :], io["cols"])

        def col(name, i):
            return cols[:, COLS[name][0] + i:COLS[name][0] + i + 1]



        units, chunks, _ = unit_plan()
        raw_tok, split_tok, used_tok = {}, {}, {}
        nxt = [0]

        def fetch(u, *after):
            if u < len(units):
                off, k, n, _ = units[u]
                src = bass.AP(tensor=io["wflat"].tensor, offset=off, ap=[[k * n, 128], [1, k * n]])
                raw_tok[u] = SP.put(S_RAW[u % NRAW], cnt, raw[u % NRAW][:, 0:k * n], src, *after)

        for u in range(NRAW):
            fetch(u)

        def split_to(u):
            while nxt[0] <= min(u, len(units) - 1):
                i = nxt[0]
                _, k, n, _ = units[i]
                r, h, l = (b[i % m][:, 0:k * n] for b, m in ((raw, NRAW), (whi, NSPL), (wlo, NSPL)))
                pe = [used_tok[i - NSPL]] if i >= NSPL else []
                ta = A.put(lambda e, r=r, h=h: e.activation(h, r, ACT.Copy), raw_tok[i], *pe)
                tv = V.put(lambda e, r=r, h=h, l=l: e.tensor_tensor(l, r, h.bitcast(F32), ALU.subtract), ta)
                split_tok[i] = tv
                fetch(i + NRAW, tv)
                nxt[0] += 1

        tasks = []

        def tick():
            for t in list(tasks):
                if next(t, "end") == "end":
                    tasks.remove(t)

        def drain(*which):
            which = which or tuple(tasks)
            while any(t in tasks for t in which):
                tick()

        def spawn(gen):
            tasks.append(gen)
            return gen

        def gemm_a(name, xs, evac, mid={}):
            ids = chunks[name]
            slots = [GR.get(), GR.get()]
            for j, u in enumerate(ids):
                _, kt, n, k0 = units[u]
                split_to(u + AHEAD)
                if j in mid:
                    mid[j]()
                hi = whi[u % NSPL][:, 0:kt * n].rearrange("p (k n) -> p k n", n=n)
                lo = wlo[u % NSPL][:, 0:kt * n].rearrange("p (k n) -> p k n", n=n)
                toks = [xs.tok[k0 + k] for k in range(kt)] + [split_tok[u]]
                if j == 0:
                    toks += slots[0].free + slots[1].free

                def mm(e, first=j == 0, last=j == len(ids) - 1, kt=kt, n=n, k0=k0, hi=hi, lo=lo):
                    for k in range(kt):
                        for t in range(2):
                            o = slots[t].ap[:, 0:n]
                            xh = xs.h(k0 + k)[:, t * 128:t * 128 + 128]
                            xl = xs.l(k0 + k)[:, t * 128:t * 128 + 128]
                            e.matmul(o, xh, hi[:, k, :], start=first and k == 0, stop=False)
                            e.matmul(o, xh, lo[:, k, :], start=False, stop=False)
                            r = e.matmul(o, xl, hi[:, k, :], start=False, stop=last and k == kt - 1)
                    return r

                tp = used_tok[u] = P.put(mm, *toks)
                tick()
            for t in range(2):
                slots[t].free = evac(t, slots[t].ap, tp)

        def gemm_b(name, xs, evac, mid={}):
            ids = chunks[name]
            n = units[ids[0]][2]
            slots = [GR.get() for _ in range(n // 256)]
            for j, u in enumerate(ids):
                _, kt, n, k0 = units[u]
                split_to(u + AHEAD)
                if j in mid:
                    mid[j]()
                hi = whi[u % NSPL][:, 0:kt * n].rearrange("p (k n) -> p k n", n=n)
                lo = wlo[u % NSPL][:, 0:kt * n].rearrange("p (k n) -> p k n", n=n)
                toks = [xs.tok[k0 + k] for k in range(kt)] + [split_tok[u]]
                if j == 0:
                    for s in slots:
                        toks += s.free

                def mm(e, first=j == 0, last=j == len(ids) - 1, kt=kt, n=n, k0=k0, hi=hi, lo=lo):
                    for f in range(n // 128):
                        o = slots[f // 2].ap[:, 256 * (f % 2):256 * (f % 2) + 256]
                        c = slice(128 * f, 128 * f + 128)
                        for k in range(kt):
                            e.matmul(o, hi[:, k, c], xs.h(k0 + k), start=first and k == 0 and f % 2 == 0,
                                     stop=False, skip_group_check=True)
                            e.matmul(o, lo[:, k, c], xs.h(k0 + k), start=False, stop=False, skip_group_check=True)
                            r = e.matmul(o, hi[:, k, c], xs.l(k0 + k), start=False,
                                         stop=last and k == kt - 1, skip_group_check=True)
                    return r

                tp = used_tok[u] = P.put(mm, *toks)
                tick()
            for i, s in enumerate(slots):
                s.free = evac(i, s.ap, tp)

        def gemm_s(name, xs, evac):
            (u,) = chunks[name]
            _, kt, n, k0 = units[u]
            split_to(u + AHEAD)
            s = GR.get()
            hi = whi[u % NSPL][:, 0:kt * n].rearrange("p (k n) -> p k n", n=n)
            lo = wlo[u % NSPL][:, 0:kt * n].rearrange("p (k n) -> p k n", n=n)

            def mm(e):
                o = s.ap[0:n, 0:T]
                for k in range(kt):
                    e.matmul(o, hi[:, k, :], xs.h(k), start=k == 0, stop=False)
                    e.matmul(o, lo[:, k, :], xs.h(k), start=False, stop=False)
                    r = e.matmul(o, hi[:, k, :], xs.l(k), start=False, stop=k == kt - 1)
                return r

            tp = used_tok[u] = P.put(mm, split_tok[u], *s.free, *xs.tok)
            s.free = evac(s.ap[0:n, 0:T], tp)
            tick()

        def to_split(dst, d0, n, src, after, scale=None):
            for f in range(0, n, 2):
                s = SR.get()

                def tr(e, f=f, s=s):
                    for i in range(2):
                        for t in range(2):
                            r = e.transpose(s.ap[:, 256 * i + 128 * t:256 * i + 128 * t + 128],
                                            src(t)[:, 128 * (f + i):128 * (f + i) + 128], ident)
                    return r

                tp = P.put(tr, t_cst, *s.free, *after)
                s.free = [split_psum(dst, d0 + f, s.ap, tp, scale and [scale(f), scale(f + 1)])]

        def split_psum(dst, k, ps, tp, scale=None):
            p2 = ps[:, :].rearrange("p (i t) -> p i t", i=2)
            f = dst.first + k
            if scale is None:
                h, l = dst.hi[:, f:f + 2, :], dst.lo[:, f:f + 2, :]
                ta = A.put(lambda e: e.activation(h, p2, ACT.Copy), tp)
                tv = V.put(lambda e: e.tensor_tensor(l, p2, h.bitcast(F32), ALU.subtract), ta)
            else:
                for i in range(2):
                    h, c, pi = dst.hi[:, f + i, :], scale[i], p2[:, i, :]
                    ta = A.put(lambda e, h=h, c=c, pi=pi: e.activation(h, pi, ACT.Identity, scale=c), tp, t_cols)
                for i in range(2):
                    h, l, c, pi = dst.hi[:, f + i, :], dst.lo[:, f + i, :], scale[i], p2[:, i, :]
                    tv = V.put(lambda e, h=h, l=l, c=c, pi=pi: e.scalar_tensor_tensor(
                        out=l, in0=pi, scalar=c, in1=h.bitcast(F32), op0=ALU.mult, op1=ALU.subtract), ta)
            dst.tok[k] = dst.tok[k + 1] = tv
            return tv

        def rstd(y, ss, n, mean, *after):
            v, w = small(n), small(n)
            t = G.put(lambda e: e.tensor_scalar(v, ss, mean, EPS, ALU.mult, ALU.add), *after)
            t = G.put(lambda e: e.tensor_tensor(y, v, expo[:, 0:n], ALU.pow), t, t_expo)
            t = V.put(lambda e: e.tensor_tensor(w, v, y, ALU.mult), t)
            t = V.put(lambda e: e.tensor_tensor(w, w, y, ALU.mult), t)
            t = V.put(lambda e: e.tensor_scalar(w, w, -0.5, 1.5, ALU.mult, ALU.add), t)
            return V.put(lambda e: e.tensor_tensor(y, y, w, ALU.mult), t)

        diag_free, junk_tok = [], []

        class Norm:

            def __init__(self, i, name, dst, src):
                self.i, self.name, self.dst, self.src = i, name, dst, src
                self.ss, self.s2, self.r = (stat[:, 8 * i + a:8 * i + b] for a, b in ((0, 4), (4, 6), (6, 8)))
                self.rT = rTs[i % 2]
                self.tok = {}

            def half(self, n, after):
                to_split(self.dst, 4 * n, 4, lambda t: self.src[:, t, 512 * n:512 * n + 512], after,
                         lambda f: col(self.name, 4 * n + f))

            def squares(self, n, after):
                for t in range(2):
                    a = A.put(lambda e, t=t: e.activation(
                        junk[:, :], self.src[:, t, 512 * n:512 * n + 512], ACT.Square,
                        accum_out=self.ss[:, 2 * n + t:2 * n + t + 1]), *after, *junk_tok)
                    junk_tok[:] = [a]
                self.tok[n] = a

            def root(self):
                t = V.put(lambda e: e.tensor_tensor(self.s2, self.ss[:, 0:2], self.ss[:, 2:4], ALU.add),
                          self.tok[0], self.tok[1])
                self.tr = rstd(self.r, self.s2, 2, 1.0 / D, t)

            def across(self):
                for t in range(2):
                    a = V.put(lambda e, t=t: e.tensor_scalar(diag[:, t, :], ident, self.r[:, t:t + 1], None, ALU.mult),
                              self.tr, t_cst, *diag_free)
                s = SR.get()

                def mm(e):
                    for t in range(2):
                        r = e.matmul(s.ap[:, 128 * t:128 * t + 128], ones[:, :], diag[:, t, :], start=True, stop=True)
                    return r

                tp = P.put(mm, a, t_ones, *s.free)
                diag_free[:] = [tp]
                self.trT = V.put(lambda e: e.tensor_copy(self.rT[:, :], s.ap[:, 0:T]), tp, V.last)
                s.free = [self.trT]

            def rest(self, wait=3):
                self.root()
                for _ in range(wait):
                    yield
                self.across()

            def wide(self, p=128, n=2):
                return self.rT[0:p, :].unsqueeze(1).to_broadcast([p, n, T])

        def everything():
            return [q.last for q in (P, A, V, G) if q.n]

        def residual_rms(name, xs, fb, w_tok, x_tok, nrm, mid={}):
            ss, s2, r = small(4), small(2), small(2)
            tok = {}
            for n in range(2):
                def evac(t, ps, tp, n=n):
                    a = A.put(lambda e: e.activation(junk[:, :], ps[:, :], ACT.Square,
                                                     accum_out=ss[:, 2 * n + t:2 * n + t + 1]), tp, *junk_tok)
                    junk_tok[:] = [a]
                    tok[n, t] = V.put(lambda e: e.tensor_tensor(
                        fb[:, t, 512 * n:512 * n + 512], ps[:, :], row[:, 512 * n:512 * n + 512], ALU.mult), a, w_tok)
                    return [tok[n, t]]
                gemm_a(f"{name}{n}", xs, evac, mid if n == 0 else {})
            tv = V.put(lambda e: e.tensor_tensor(s2, ss[:, 0:2], ss[:, 2:4], ALU.add), tok[1, 1])
            tr = rstd(r, s2, 2, 1.0 / D, tv)
            out, both = [None, None], []
            for n in range(2):
                for t in range(2):
                    xx, ff = x[:, t, 512 * n:512 * n + 512], fb[:, t, 512 * n:512 * n + 512]
                    out[t] = V.put(lambda e, xx=xx, ff=ff, t=t: e.scalar_tensor_tensor(
                        out=xx, in0=ff, scalar=r[:, t:t + 1], in1=xx, op0=ALU.mult, op1=ALU.add),
                        tr, tok[n, t], x_tok[t])
                both.append(list(out))
            for n in range(2):
                nrm.half(n, both[n])
            for n in range(2):
                nrm.squares(n, both[n])
            spawn(nrm.rest())
            return out

        def residual(name, xs, factor, x_tok, nrm, mid={}):
            out = [None, None]

            def rest(n, toks, last):
                if not last:
                    yield
                nrm.half(n, toks)
                nrm.squares(n, toks)
                if last:
                    yield from nrm.rest()

            for n in range(2):
                def evac(t, ps, tp, n=n):
                    xx = x[:, t, 512 * n:512 * n + 512]
                    out[t] = V.put(lambda e: e.scalar_tensor_tensor(
                        out=xx, in0=ps[:, :], scalar=factor, in1=xx, op0=ALU.mult, op1=ALU.add), tp, x_tok[t])
                    return [out[t]]
                gemm_a(f"{name}{n}", xs, evac, mid if n == 0 else {})
                if n == 0 and nrm:
                    spawn(rest(0, list(out), False))
            drain()
            return list(out), rest(1, list(out), True) if nrm else None

        hT = Split(hT_hi, hT_lo, 0, 8)

        def start(gen):
            spawn(gen)
            tick()

        def ffn(tag, nrm, mid, finish):
            ph = Phase(tag)
            hid_hi = ph.new("hid_hi", [128, 22, T], F32R)
            hid_lo = ph.new("hid_lo", [128, 22, T], F32R)
            sg = [ph.new(f"sg{i}", [128, 2, T]) for i in range(2)]
            hh = [ph.new(f"hh{i}", [128, 2, T]) for i in range(2)]
            fb = ph.new("fb", [128, 2, D])
            assert ph.off <= m2_late
            hid = Split(hid_hi, hid_lo, 0, 22)
            here = everything()
            hh_free = [here, here]

            def turn(c, ta, tv):
                yield
                h = hh[c % 2][:, :, :]
                tv = V.put(lambda e: e.tensor_tensor(h, h, sg[c % 2][:, :, :], ALU.mult), ta, tv)
                hi, lo = hid_hi[:, 2 * c:2 * c + 2, :], hid_lo[:, 2 * c:2 * c + 2, :]
                ta = A.put(lambda e: e.activation(hi, h, ACT.Copy), tv, *here)
                yield
                tv = V.put(lambda e: e.tensor_tensor(lo, h, hi.bitcast(F32), ALU.subtract), ta)
                hid.tok[2 * c] = hid.tok[2 * c + 1] = tv
                hh_free[c % 2] = [tv]

            for c in range(11):
                tok = {}

                def evac(i, ps, tp, c=c, tok=tok):
                    b = (sg, hh)[i][c % 2][:, :, :]
                    p2 = ps[:, :].rearrange("p (i t) -> p i t", i=2)
                    tv = V.put(lambda e: e.tensor_tensor(b, p2, nrm.wide(), ALU.mult), tp, nrm.trT, *hh_free[c % 2])
                    if i == 0:
                        tok["a"] = A.put(lambda e: e.activation(b, b, ACT.Silu), tv)
                    tok["v"] = tv
                    return [tv]

                gemm_b(f"{tag}gu{c}", hT, evac, mid if c == 0 else {})
                spawn(turn(c, tok["a"], tok["v"]))
            return finish(f"{tag}dn", hid, fb, {10: drain})

        def softmax_block(ph_P, mx, sums, heads, L, after):
            nm = small(heads)
            t = V.put(lambda e: e.tensor_scalar(nm, mx, -1.0, None, ALU.mult), *after)
            for h in range(heads):
                t = A.put(lambda e, h=h: e.activation(ph_P[:, h, 0:L], ph_P[:, h, 0:L], ACT.Exp,
                                                      bias=nm[:, h:h + 1], accum_out=sums[:, h:h + 1]), t)
            return t

        def attention(Pb, PT, score, bias, value, after, vtok, out, prior=(), order=(0, 2, 4, 6, 1, 3, 5, 7)):
            p_free = list(prior)
            for qb in range(2):
                L = 128 * (qb + 1)
                mx, sums, rec = small(8), small(8), small(8)
                per = 512 // L
                for g in range(0, 8, per):
                    hs = order[g:g + per]
                    s = SR.get()

                    def mm(e, s=s, hs=hs, qb=qb, L=L):
                        for i, h in enumerate(hs):
                            r = score(e, s.ap[:, i * L:i * L + L], h, qb, L)
                        return r

                    tp = P.put(mm, *s.free, *after)
                    for i, h in enumerate(hs):
                        tv = V.put(lambda e, s=s, i=i, h=h, qb=qb, L=L, mx=mx: e.tensor_tensor_reduce(
                            Pb[:, h, 0:L], s.ap[:, i * L:i * L + L], bias(qb, h), 1.0, -3.0e38,
                            ALU.add, ALU.max, mx[:, h:h + 1]), tp, *p_free)
                    s.free = [tv]
                    if g % 4 == 2 or per == 4:
                        yield
                te = softmax_block(Pb, mx, sums, 8, L, [tv])
                tr = V.put(lambda e, rec=rec, sums=sums: e.reciprocal(rec, sums), te)
                yield
                if qb:
                    yield
                blocks = [(h, k) for h in range(8) for k in range(qb + 1)]
                for b in range(0, len(blocks), 4):
                    s = SR.get()

                    def tr4(e, s=s, b=b, blocks=blocks):
                        for i, (h, k) in enumerate(blocks[b:b + 4]):
                            r = e.transpose(s.ap[:, 128 * i:128 * i + 128], Pb[:, h, 128 * k:128 * k + 128], ident)
                        return r

                    tp = P.put(tr4, te, *s.free)
                    if b % 8 == 0:
                        tc = A.put(lambda e, s=s, b=b: e.activation(
                            PT[:, b:b + 4, :], s.ap[:, :].rearrange("p (i t) -> p i t", i=4), ACT.Copy), tp)
                    else:
                        tc = V.put(lambda e, s=s, b=b: e.tensor_copy(
                            PT[:, b:b + 4, :], s.ap[:, :].rearrange("p (i t) -> p i t", i=4)), tp)
                    s.free = [tc]
                p_free = [tp]
                ends = [A.last, V.last]
                yield
                if not qb:
                    yield
                s = SR.get()

                def pv(e, s=s, qb=qb):
                    for h in range(8):
                        for k in range(qb + 1):
                            r = e.matmul(s.ap[:, 64 * h:64 * h + 64], PT[:, h * (qb + 1) + k, :], value(h, k),
                                         start=k == 0, stop=k == qb)
                    return r

                tp = P.put(pv, *ends, *vtok, *s.free)
                s.free = out(qb, s.ap[:, :].rearrange("p (h d) -> p h d", h=8), rec, [tp, tr])
                yield

        def spread(ap, n):
            return ap.unsqueeze(2).to_broadcast([128, ap.shape[1], n])

        m1 = Phase("m1")
        br_hi, br_lo = m1.new("br_hi", [128, 8, T], F32R), m1.new("br_lo", [128, 8, T], F32R)
        gates = m1.new("gates", [128, 2, 3072])
        r1 = m1.off
        m1.new("r1a", [128, 2, D])
        m1.new("r1b", [128, 1152])
        gv, gr = m1.new("gv", [128, 2, 512]), m1.new("gr", [128, 2, 512])
        mq, mk = m1.new("mq", [128, 4, T]), m1.new("mk", [128, 4, T])
        mv = m1.new("mv", [128, 2, 512])
        pu = m1.new("pu", [128, 4, 16 + T])
        gqk_off = m1.off
        gqk = m1.new("gqk", [128, 4, T])
        bcum = m1.new("bcum", [128, 2, T])
        r2 = m1.off
        lE = m1.new("lE", [128, 8, T])
        lQ = m1.new("lQ", [128, 8, T])
        lK = m1.new("lK", [128, 8, T])
        acc_off = m1.off
        acc = m1.new("acc", [128, 3, 4, 128])
        msk = m1.new("msk", [128, 8, 128], U8)
        wg2 = m1.new("wg2", [128, 256])
        wpl = m1.new("wpl", [128, 4, 128])
        g1T = m1.new("g1T", [128, 256])
        gnw = m1.new("gnw", [128, 128])
        t1 = m1.new("t1", [128, 4, 272], off=r1)
        t2 = m1.new("t2", [128, 4, 272], off=r1 + 4352)
        pp = m1.new("pp", [128, 4, T], off=r1 + 8704)
        mixed = m1.new("mixed", [128, 2, D], off=r1)
        mtmp = m1.new("mtmp", [128, 2, 512], off=r1 + 8192)
        lmn = m1.new("lmn", [128, 2, T], off=acc_off)
        lab = m1.new("lab", [128, 2, T], off=acc_off + 2048)
        yc = m1.new("yc", [128, 2, 512], off=gqk_off)
        Pb = m1.new("Pb", [128, 8, T], off=r2)
        PT = m1.new("PT", [128, 16, 128], off=r2 + 8192)
        fb1 = m1.new("fb", [128, 2, D], off=r2)
        mskf = m1.new("mskf", [128, D], off=r2)
        alibi = m1.new("alibi", [128, 8 * 384], off=r2 + 16384)

        t_msk = load(AD, "msk", mskf[:, :], io["c_masks"])
        t_wg2 = load(AD, "wg2", wg2[0:16, :], io["gla_w_g2"].rearrange("a r c -> (a r) c"))
        t_wpl = load(AD, "wpl", wpl[:, :, :], io["pool_w"].rearrange("a g c d -> c (a g) d"))
        t_gnw = load(AD, "gnw", gnw[:, :], bcast(io["gla_norm"], 128))
        t_row = load(AD, "row", row[:, :], bcast(io["norm_mix_post"], D))

        t_expo = G.put(lambda e: e.memset(expo[:, :], -0.5))
        t_ones = V.put(lambda e: e.memset(ones[:, :], 1.0))
        nm1 = Norm(0, "norm_mix_pre", hT, x)
        A.put(lambda e: e.activation(junk[:, 0:1], ones[:, 0:1], ACT.Copy), t_ones)
        nm1.half(0, t_x)
        split_to(0)
        nm1.half(1, t_x)
        split_to(AHEAD)
        junk_tok[:] = [A.last]
        for n in range(2):
            nm1.squares(n, t_x)
        spawn(nm1.rest())
        done = {}

        def evac_gqk(i, ps, tp):
            o = gqk[:, 2 * i:2 * i + 2, :]
            p2 = ps[:, :].rearrange("p (i t) -> p i t", i=2)
            done["gqk", i] = V.put(lambda e: e.scalar_tensor_tensor(
                out=o, in0=p2, scalar=0.125 if i == 0 else 1.0, in1=nm1.wide(), op0=ALU.mult, op1=ALU.mult),
                tp, nm1.trT)
            return [done["gqk", i]]

        br = Split(br_hi, br_lo, 0, 8)
        brc = Split(hT_hi, hT_lo, 0, 4)
        first = {}

        def gla():
            t_mask = V.put(lambda e: e.tensor_copy(msk[:, :, :], mskf[:, :].rearrange("p (l t) -> p l t", l=8)), t_msk)
            s2 = SR.get()

            def lg(e):
                for f in range(2):
                    r = e.matmul(s2.ap[:, 256 * f:256 * f + 256], wg2[0:16, 128 * f:128 * f + 128], g1T[0:16, :],
                                 start=True, stop=True)
                return r

            tp = P.put(lg, first["g1"], t_wg2, *s2.free)
            yield
            for f in range(2):
                z = s2.ap[:, 256 * f:256 * f + 256]
                ta = A.put(lambda e, f=f, z=z: e.activation(lab[:, f, :], z, ACT.Abs, bias=col("gla_b_g", f)), tp, t_cols)
            for f in range(2):
                z = s2.ap[:, 256 * f:256 * f + 256]
                tv = V.put(lambda e, f=f, z=z: e.tensor_scalar(lmn[:, f, :], z, col("gla_b_g", f), 0.0,
                                                               ALU.add, ALU.min), ta, t_cols)
            s2.free = [ta, tv]
            yield
            ta = A.put(lambda e: e.activation(lab[:, :, :], lab[:, :, :], ACT.Exp, scale=-1.0), ta)
            ta = A.put(lambda e: e.activation(lab[:, :, :], lab[:, :, :], ACT.Ln, bias=1.0), ta)
            yield
            tv = V.put(lambda e: e.tensor_tensor(lmn[:, :, :], lmn[:, :, :], lab[:, :, :], ALU.subtract), ta, tv)
            for f in range(2):
                ts = V.put(lambda e, f=f: e.tensor_tensor_scan(bcum[:, f, :], cst[:, C_RST:C_RST + 256], lmn[:, f, :],
                                                               0.0, ALU.mult, ALU.add), tv, t_rest)
            tz = V.put(lambda e: e.memset(acc[:, :, :, :], 0.0), ts)
            yield
            free_l = []
            for pr in range(2):
                b = bcum[:, pr, :]
                for i, m in enumerate(MASKS):
                    bv = b.rearrange("p (n c) -> p n c", c=2 * m)
                    ev = lE[:, i, :].rearrange("p (n c) -> p n c", c=2 * m)
                    nb = T // (2 * m)
                    ref = bv[:, :, m - 1:m].to_broadcast([128, nb, m])
                    tv = G.put(lambda e, bv=bv, ev=ev, ref=ref, m=m: e.tensor_tensor(
                        ev[:, :, 0:m], ref, bv[:, :, 0:m], ALU.subtract), ts, *free_l)
                    if m < 64:
                        tv = G.put(lambda e, bv=bv, ev=ev, ref=ref, m=m: e.tensor_tensor(
                            ev[:, :, m:2 * m], bv[:, :, m:2 * m], ref, ALU.subtract), ts)
                    else:
                        tv = G.put(lambda e, bv=bv, ev=ev, m=m: e.tensor_copy(
                            ev[:, :, m:2 * m], bv[:, :, m:2 * m]), ts)
                sb0 = small(1)
                t0 = G.put(lambda e, b=b, sb0=sb0: e.tensor_tensor(sb0, b[:, 63:64], b[:, 127:128], ALU.add), ts)
                G.put(lambda e, b=b: e.tensor_scalar(lE[:, 7, 64:128], b[:, 64:128], -1.0, b[:, 127:128],
                                                     ALU.mult, ALU.add), ts)
                G.put(lambda e, b=b: e.tensor_copy(lE[:, 7, 128:192], b[:, 128:192]), ts)
                G.put(lambda e, b=b: e.tensor_scalar(lE[:, 7, 192:256], b[:, 192:256], b[:, 191:192], None, ALU.add), ts)
                tv = G.put(lambda e, b=b, sb0=sb0: e.tensor_scalar(lE[:, 7, 0:64], b[:, 0:64], -1.0, sb0,
                                                                   ALU.mult, ALU.add), t0)
                yield
                ta = A.put(lambda e: e.activation(lE[:, :, :], lE[:, :, :], ACT.Exp, scale=1.0 / 16), tv)
                yield
                yield
                for dst, src in ((lQ, gqk[:, pr, :]), (lK, gqk[:, 2 + pr, :])):
                    wide = src.unsqueeze(1).to_broadcast([128, 8, T])
                    tq = G.put(lambda e, dst=dst, wide=wide: e.tensor_tensor(dst[:, :, :], wide, lE[:, :, :], ALU.mult),
                               ta, done["gqk", 0], done["gqk", 1], *free_l)
                yield
                yield
                yield
                for par in range(2):
                    pa = slice(64 * par, 64 * par + 64)
                    h = 2 * pr + par
                    for j in range(2):
                        for half in range(2):
                            s = SR.get()

                            def lv(e, s=s, pa=pa, j=j, half=half, pr=pr):
                                for i in range(4):
                                    l = 4 * half + i
                                    w = slice(128 * j, 128 * j + 128)
                                    kk, qq = (lK[pa, l, w], lQ[pa, l, w]) if l < 7 else (gqk[pa, 2 + pr, w], gqk[pa, pr, w])
                                    r = e.matmul(s.ap[:, 128 * i:128 * i + 128], kk, qq, start=True, stop=True)
                                return r

                            tp = P.put(lv, tq, *s.free)
                            for i in range(4):
                                tv = V.put(lambda e, s=s, i=i, j=j, h=h, half=half: e.copy_predicated(
                                    acc[:, j, h, :], msk[:, 4 * half + i, :], s.ap[:, 128 * i:128 * i + 128]), tp, tz, t_mask, tv)
                            s.free = [tv]
                        yield
                    s = SR.get()
                    tp = P.put(lambda e, s=s, pa=pa: e.matmul(s.ap[:, 0:128], lK[pa, 7, 0:128], lQ[pa, 7, 128:256],
                                                              start=True, stop=True), tq, *s.free)
                    tv = A.put(lambda e, s=s, h=h: e.activation(acc[:, 2, h, :], s.ap[:, 0:128], ACT.Copy), tp, tz)
                    s.free = [tv]
                free_l = [tp]
            done["levels"] = tp
            ends = [A.last, V.last]
            yield
            for j in range(2):
                s = SR.get()

                def ov(e, s=s, j=j):
                    for h in range(4):
                        o = s.ap[:, 128 * h:128 * h + 128]
                        if j:
                            e.matmul(o, acc[:, 2, h, :], gv[:, 0, 128 * h:128 * h + 128], start=True, stop=False)
                        r = e.matmul(o, acc[:, j, h, :], gv[:, j, 128 * h:128 * h + 128], start=j == 0, stop=True)
                    return r

                tp = P.put(ov, *ends, done["gv"], *s.free)
                ss = small(4)
                for h in range(4):
                    ta = A.put(lambda e, s=s, h=h, j=j, ss=ss: e.activation(
                        lE[:, 4 * j + h, 0:128], s.ap[:, 128 * h:128 * h + 128], ACT.Square, accum_out=ss[:, h:h + 1]),
                        tp, done["levels"])
                r = small(4)
                tr = rstd(r, ss, 4, 1.0 / 128, ta)
                o3 = s.ap[:, :].rearrange("p (h d) -> p h d", h=4)
                tmp = lK[:, 2 * j:2 * j + 2, :].rearrange("p a (b d) -> p (a b) d", d=128)
                tv = V.put(lambda e, o3=o3, r=r, tmp=tmp: e.tensor_tensor(tmp, o3, spread(r, 128), ALU.mult), tr, done["levels"])
                s.free = [tv]
                g4 = gr[:, j, :].rearrange("p (h d) -> p h d", h=4)
                tv = V.put(lambda e, g4=g4, tmp=tmp: e.tensor_tensor(g4, tmp, g4, ALU.mult), tv, first["gr"])
            yield
            to_split(br, 0, 4, lambda t: gr[:, t, :], [tv])
            done["gla"] = [A.last, V.last, P.last]

        def pool():
            t0 = done["pu"]
            z = G.put(lambda e: e.memset(t1[:, :, 0:16], 0.0))
            z = G.put(lambda e: e.memset(t2[:, :, 0:16], 0.0))
            t = G.put(lambda e: e.tensor_tensor(t1[:, :, 1:272], pu[:, :, 1:272], pu[:, :, 0:271], ALU.add), z, *t0)
            t = G.put(lambda e: e.tensor_tensor(t2[:, 1:4, 3:272], t1[:, 1:4, 3:272], t1[:, 1:4, 1:270], ALU.add), t)
            yield
            t = G.put(lambda e: e.tensor_tensor(t1[:, 2:4, 7:272], t2[:, 2:4, 7:272], t2[:, 2:4, 3:268], ALU.add), t)
            t = G.put(lambda e: e.tensor_tensor(t2[:, 3, 15:272], t1[:, 3, 15:272], t1[:, 3, 7:264], ALU.add), t)
            inv = small(64)
            for g in range(4):
                src = (t1, t2)[g % 2]
                tw = V.put(lambda e, g=g, src=src: e.scalar_tensor_tensor(
                    out=pp[:, g, :], in0=src[:, g, 16:272], scalar=1.0 / (2 << g), in1=pu[:, g, 16:272],
                    op0=ALU.mult, op1=ALU.subtract), t)
                t3 = G.put(lambda e, g=g, src=src: e.tensor_tensor(
                    inv[:, 16 * g:16 * g + 16], src[:, g, 16:32], cst[:, C_INV + 16 * g:C_INV + 16 * g + 16], ALU.mult), t, t_rest)
            yield
            for g in range(4):
                t = G.put(lambda e, g=g: e.tensor_tensor(pp[:, g, 0:16], inv[:, 16 * g:16 * g + 16], pu[:, g, 16:32],
                                                         ALU.subtract), t3, tw)
            yield
            yield
            for g in range(0, 4, 2):
                s = SR.get()

                def pm(e, s=s, g=g):
                    for i in range(2):
                        r = e.matmul(s.ap[:, 256 * i:256 * i + 256], wpl[:, g + i, :], pp[:, g + i, :], start=True, stop=True)
                    return r

                tp = P.put(pm, t, tw, t_wpl, *s.free)
                s.free = [split_psum(br, 4 + g, s.ap, tp, [col("pool_scale", g), col("pool_scale", g + 1)])]
            done["pool"] = [P.last]

        def moba():
            t_alibi = load(SP, "alibi", alibi[:, :], io["c_alibi"], *done["gla"])
            for _ in range(3):
                yield

            def score(e, ps, h, qb, L):
                pa = slice(64 * (h % 2), 64 * (h % 2) + 64)
                return e.matmul(ps, mq[pa, h // 2, 128 * qb:128 * qb + 128], mk[pa, h // 2, 0:L], start=True, stop=True)

            def bias(qb, h):
                o, L = (0, 128) if qb == 0 else (1024, 256)
                return alibi[:, o + L * h:o + L * h + L]

            def out(qb, ps, rec, after):
                o = yc[:, qb, :].rearrange("p (h d) -> p h d", h=8)
                t = V.put(lambda e: e.tensor_tensor(o, ps, spread(rec, 64), ALU.mult), *after, *done["gla"])
                done["yc"] = t
                return [t]

            yield from attention(Pb, PT, score, bias, lambda h, k: mv[:, k, 64 * h:64 * h + 64],
                                 [done["mq"], done["mk"], t_alibi], [done["mv"]], out, done["gla"])
        gemm_b("qk", hT, evac_gqk)

        def evac_tm(key, out, nrm):
            def evac(t, ps, tp):
                o = out[:, t, :]
                done[key] = A.put(lambda e: e.activation(o, ps[:, 0:o.shape[-1]], ACT.Identity, scale=nrm.r[:, t:t + 1]),
                                  tp, nrm.tr)
                return [done[key]]
            return evac

        def evac_g1(ps, tp):
            first["g1"] = V.put(lambda e: e.tensor_tensor(g1T[0:16, :], ps, nm1.rT[0:16, :], ALU.mult), tp, nm1.trT)
            return [first["g1"]]

        gemm_s("g1", hT, evac_g1)
        gemm_a("gv", hT, evac_tm("gv", gv, nm1))
        t_gla = spawn(gla())
        tgr = []

        def evac_gr(t, ps, tp):
            a = A.put(lambda e: e.activation(gr[:, t, :], ps[:, :], ACT.Silu, scale=nm1.r[:, t:t + 1]), tp, nm1.tr)
            g4 = gr[:, t, :].rearrange("p (h d) -> p h d", h=4)
            first["gr"] = V.put(lambda e: e.tensor_tensor(
                g4, g4, gnw[:, :].unsqueeze(1).to_broadcast([128, 4, 128]), ALU.mult), a, t_gnw)
            return [a]

        gemm_a("gr", hT, evac_gr)

        z_pu = V.put(lambda e: e.memset(pu[:, :, 0:16], 0.0))
        done["pu"] = [z_pu]

        def evac_pu(i, ps, tp):
            p2 = ps[:, :].rearrange("p (i t) -> p i t", i=2)
            a = V.put(lambda e: e.tensor_tensor(pu[:, 2 * i:2 * i + 2, 16:272], p2, nm1.wide(), ALU.mult), tp, nm1.trT)
            done["pu"].append(a)
            return [a]

        def keep_b(key, out, nrm, scale=1.0):
            def evac(i, ps, tp):
                p2 = ps[:, :].rearrange("p (i t) -> p i t", i=2)
                done[key] = V.put(lambda e: e.scalar_tensor_tensor(
                    out=out[:, 2 * i:2 * i + 2, :], in0=p2, scalar=scale, in1=nrm.wide(), op0=ALU.mult, op1=ALU.mult),
                    tp, nrm.trT)
                return [done[key]]
            return evac

        gemm_b("pu", hT, evac_pu)
        spawn(pool())
        gemm_b("mq", hT, keep_b("mq", mq, nm1, 0.125))
        gemm_b("mk", hT, keep_b("mk", mk, nm1))

        gemm_a("mv", hT, evac_tm("mv", mv, nm1))
        t_moba = None
        gtok = {}
        for n in range(6):
            def evac(t, ps, tp, n=n):
                gtok[n, t] = A.put(lambda e: e.activation(gates[:, t, 512 * n:512 * n + 512], ps[:, :], ACT.Sigmoid,
                                                           scale=nm1.r[:, t:t + 1]), tp, nm1.tr)
                return [gtok[n, t]]
            gemm_a(f"gt{n}", hT, evac)
            if t_moba is None and not any(q is t_gla for q in tasks):
                t_moba = spawn(moba())
        drain()
        if t_moba is None:
            t_moba = spawn(moba())
            drain()
        mt = {}

        def mixed_first():
            yield
            to_split(br, 0, 4, lambda t: mixed[:, t, 0:512], [mt[0, 0], mt[1, 0]])

        def mixed_second():
            to_split(br, 4, 4, lambda t: mixed[:, t, 512:1024], [mt[0, 1], mt[1, 1]])

        def branch(i, xs, k0):
            sub = Split(xs.hi, xs.lo, xs.first + k0, 4)
            sub.tok = xs.tok[k0:k0 + 4]
            for n in range(2):
                def evac(t, ps, tp, n=n):
                    gsl = gates[:, t, 1024 * i + 512 * n:1024 * i + 512 * n + 512]
                    mx = mixed[:, t, 512 * n:512 * n + 512]
                    if i == 0:
                        mt[t, n] = V.put(lambda e: e.tensor_tensor(mx, ps[:, :], gsl, ALU.mult), tp,
                                         gtok[2 * i + n, t], *done["pool"])
                        return [mt[t, n]]
                    a = V.put(lambda e: e.tensor_tensor(mtmp[:, t, :], ps[:, :], gsl, ALU.mult), tp,
                              gtok[2 * i + n, t], *mt.get(("f", t), []))
                    mt[t, n] = V.put(lambda e: e.tensor_tensor(mx, mx, mtmp[:, t, :], ALU.add), a, mt[t, n])
                    mt["f", t] = [mt[t, n]]
                    return [a]
                gemm_a(f"br{i}{n}", sub, evac)
                if (i, n) == (2, 0):
                    spawn(mixed_first())

        branch(0, br, 0)
        to_split(brc, 0, 4, lambda t: yc[:, t, :], [done["yc"]])
        branch(1, br, 4)
        branch(2, brc, 0)
        drain()
        here = everything()
        A.wait(here)
        nm_f0 = Norm(1, "norm_ffn_pre", hT, x)
        x_tok = residual_rms("wo", br, fb1, t_row, t_x, nm_f0, {2: mixed_second})

        nm_f1 = Norm(2, "ffn1_norm_2", hT, x)

        def fin0(name, hid, fb, mid):
            t_row2 = load(SP, "row2", row[:, :], bcast(io["norm_ffn_post"], D), *x_tok)
            return residual_rms(name, hid, fb, t_row2, x_tok, nm_f1, mid)

        x_tok = ffn("f0", nm_f0, {}, fin0)
        nm_m2 = Norm(3, "mix_norm_2", hT, x)
        early = everything()
        x_tok, left = ffn("f1", nm_f1, {}, lambda name, hid, fb, mid: residual(name, hid, 0.5, x_tok, nm_m2, mid))

        m2 = Phase("m2")
        ck_off = m2.off
        qf, kf = m2.new("qf", [128, 4, T]), m2.new("kf", [128, 4, T])
        vf = m2.new("vf", [128, 2, 512])
        sel = m2.new("sel", [128, 8, 128])
        ckT = m2.new("ckT", [128, 8, T], off=ck_off)
        cv = m2.new("cv", [128, 2, D], off=ck_off + 8192)
        memx = m2.new("memx", [128, 2, D], off=m2.off)
        Pb2 = m2.new("Pb", [128, 8, T])
        PT2 = m2.new("PT", [128, 16, 128])
        w1_off = m2.off
        w1 = [m2.new(f"w1{i}", [128, 16, 256], off=w1_off + 16384 * i) for i in range(2)]
        y2 = m2.new("y", [128, 2, D])
        ytmp = m2.new("ytmp", [128, 2, 512])
        PcT = m2.new("PcT", [128, 8, 128])
        gg = m2.new("gg", [128, 2, 2048])
        u_hi, u_lo = m2.new("u_hi", [128, 8, T], F32R), m2.new("u_lo", [128, 8, T], F32R)
        qn = m2.new("qn", [128, 4, T])
        ksw = m2.new("ksw", [128, 2, T])
        vsw = m2.new("vsw", [128, 2, 256])
        rel = m2.new("rel", [128, 8 * 384])
        r_off = m2.off
        R = [m2.new(f"R{i}", [128, 16, 2, 15]) for i in range(2)]
        otmp = m2.new("otmp", [128, 8, 64], off=r_off)
        w2k = m2.new("w2k", [128, 2, 128])
        w2v = m2.new("w2v", [128, 2, 64])
        gel = [m2.new(f"gel{i}", [128, 2, 30]) for i in range(2)]
        Pc = m2.new("Pc", [128, 8, 16], off=m2.off)
        ps_nat = m2.new("pos", [128, 2, 128])
        posT = m2.new("posT", [128, 2, 16])
        kcT = m2.new("kcT", [128, 32])
        vc = m2.new("vc", [128, 2, 64])
        gf = m2.new("gf", [128, 2, 32])
        gfT = m2.new("gfT", [128, T])
        onsa, ofox = m2.new("onsa", [128, 2, 512]), m2.new("ofox", [128, 2, 512])
        fx = m2.new("fx", [128, 3, 256], off=m2.off)
        hot = m2.new("hot", [128, 512])
        tbl = m2.new("tbl", [128, 8])
        Xr = m2.new("Xr", [128, 512])
        scr = nc.dram_tensor("scratch", [8, 512], F32).ap()
        wide = nc.dram_tensor("wide", [128, 4096], F32).ap()

        here = everything()
        lp = [load(SP, f"pos{i}", ps_nat[0:16, i, :], io[n].rearrange("a (i r) d -> (a i) (r d)", r=2), *early)
              for i, n in enumerate(("cmp_pos_k_2", "cmp_pos_v_2"))]
        t_hot = load(SP, "hot", hot[0:33, :], io["c_hot"], *early)
        t_tbl = load(SP, "tbl", tbl[0:32, :], io["rel_bias_table_2"], *early)
        l2 = [load(SP, f"w2k{i}", w2k[:, :, 64 * i:64 * i + 64], io["cmp_k_w2_2"].rearrange("a (k p) d -> p (a k) d", p=128),
                   *early) for i in range(2)]
        l2.append(load(SP, "w2v", w2v[:, :, :], io["cmp_v_w2_2"].rearrange("a (k p) d -> p (a k) d", p=128)))
        tz = V.put(lambda e: e.memset(tbl[32:33, :], NEG))

        def rel_bias():
            yield
            s = SR.get()

            def tr(e):
                for i in range(2):
                    r = e.transpose(s.ap[:, 16 * i:16 * i + 16], ps_nat[0:16, i, :], ident[0:16, 0:16])
                return r

            tp = P.put(tr, *lp, *s.free)
            done["posT"] = V.put(lambda e: e.tensor_copy(posT[:, :, :], s.ap[:, 0:32].rearrange("p (i r) -> p i r", i=2)), tp)
            s.free = [done["posT"]]
            s0 = SR.get()
            tp = P.put(lambda e: e.matmul(s0.ap[0:8, :], tbl[0:33, :], hot[0:33, :], start=True, stop=True),
                       t_hot, t_tbl, tz, *s0.free)
            tv = V.put(lambda e: e.tensor_copy(Xr[0:8, :], s0.ap[0:8, :]), tp)
            s0.free = [tv]
            td = load(SP, "scr", scr, Xr[0:8, :], tv)
            for _ in range(3):
                yield
            td = load(SP, "wide", wide, bcast(scr, 4096), td)
            for _ in range(3):
                yield
            done["rel"] = []
            for qb in range(2):
                L = 128 * (qb + 1)
                src = bass.AP(tensor=wide.tensor, offset=255 - 128 * qb, ap=[[4095, 128], [512, 8], [1, L]])
                dst = rel[:, (0, 1024)[qb]:(1024, 3072)[qb]].rearrange("p (h k) -> p h k", h=8)
                done["rel"].append(load(SP, f"rel{qb}", dst, src, td))

        mT = Split(u_hi, u_lo, 0, 8)
        t_mem = load(SP, "mem", memx[:, :, :], io["mem_2"].rearrange("a (k p) d -> p (a k) d", p=128), *here)
        t_sel = load(SP, "sel", sel[0:8, :, :], io["c_sel"].rearrange("k (h i) -> k h i", h=8), *here)
        nm_mk = Norm(4, "mem_kv_norm_2", mT, memx)

        def memory():
            for _ in range(6):
                yield
            for n in range(2):
                nm_mk.half(n, [t_mem])
                nm_mk.squares(n, [t_mem])
                yield
            yield from nm_mk.rest()

        lw = [[], []]

        def load_w1():
            for _ in range(8):
                yield
            for i, n in enumerate(("cmp_k_w1_2", "cmp_v_w1_2")):
                src = io[n].rearrange("a (i p) h -> p (a i) h", p=128)
                for j in range(0, 16, 4):
                    lw[i].append(load(SP, f"w1{i}{j}", w1[i][:, j:j + 4, :], src[:, j:j + 4, :], *here))
                    yield

        spawn(rel_bias())
        t_memory = spawn(memory())
        spawn(load_w1())

        def evac_kv(i, ps, tp):
            p2 = ps[:, :].rearrange("p (i t) -> p i t", i=2)
            tp = V.put(lambda e: e.tensor_tensor(p2, p2, nm_m2.wide(), ALU.mult), tp, nm_m2.trT)
            for g in range(2):
                for half in range(2):
                    pa = slice(64 * half, 64 * half + 64)
                    src = ps[pa, 256 * g + half:256 * g + 256:2].rearrange("p (c j) -> p j c", j=8)
                    for top_half in range(2):
                        sv = src[:, :, top_half:top_half + 15]
                        o = R[i][pa, 8 * top_half:8 * top_half + 8, g, :]
                        pt = posT[pa, i, 8 * top_half:8 * top_half + 8].unsqueeze(2).to_broadcast([64, 8, 15])
                        t = V.put(lambda e, o=o, sv=sv, pt=pt: e.tensor_tensor(o, sv, pt, ALU.add), tp, done["posT"], *here)
            done["R", i] = t
            return [t]

        def bound_rel(qb, h):
            o, L = (0, 128) if qb == 0 else (1024, 256)
            return rel[:, o + L * h:o + L * h + L]

        def tile_of(h):
            return slice(64 * (h // 4), 64 * (h // 4) + 64), h % 4

        def nsa():
            for i in range(2):
                s = SR.get()

                def c1(e, s=s, i=i):
                    for f in range(2):
                        for j in range(16):
                            r = e.matmul(s.ap[:, 32 * f:32 * f + 30], w1[i][:, j, 128 * f:128 * f + 128],
                                         R[i][:, j, :, :].rearrange("p g c -> p (g c)"), start=j == 0, stop=j == 15)
                    return r

                tp = P.put(c1, done["R", i], *lw[i], *s.free)
                ta = A.put(lambda e, s=s, i=i: e.activation(
                    gel[i][:, :, :], s.ap[:, 0:64].rearrange("p (f c) -> p f c", f=2)[:, :, 0:30],
                    ACT.Gelu_apprx_tanh), tp)
                s.free = [ta]
                yield
            s = SR.get()

            def c2(e, s=s):
                for f in range(2):
                    r = e.matmul(s.ap[:, 0:30], w2k[:, f, :], gel[0][:, f, :], start=f == 0, stop=f == 1)
                for g in range(2):
                    for f in range(2):
                        r = e.matmul(s.ap[0:15, 64 + 64 * g:128 + 64 * g], gel[1][:, f, 15 * g:15 * g + 15], w2v[:, f, :],
                                     start=f == 0, stop=f == 1)
                return r

            tp = P.put(c2, ta, *l2, *s.free)
            for g in range(2):
                pa = slice(64 * g, 64 * g + 64)
                V.put(lambda e, pa=pa, g=g, s=s: e.tensor_copy(kcT[pa, 0:15], s.ap[pa, 15 * g:15 * g + 15]), tp)
            tk = V.put(lambda e, s=s: e.tensor_copy(vc[0:15, :, :], s.ap[0:15, 64:192].rearrange("p (g d) -> p g d", g=2)), tp)
            s.free = [tk]
            yield
            tco = None
            for qb in range(2):
                n = (7, 15)[qb]
                o_rel, L = (0, 128) if qb == 0 else (1024, 256)
                mx, sums, rec = small(8), small(8), small(8)
                tps = []
                ss = [SR.get(), SR.get()]

                def sc(e, ss=ss, qb=qb, n=n):
                    for h in range(8):
                        pa, ti = tile_of(h)
                        r = e.matmul(ss[h // 4].ap[:, 16 * ti:16 * ti + n], qn[pa, ti, 128 * qb:128 * qb + 128],
                                     kcT[pa, 0:n], start=True, stop=True)
                    return r

                tp = P.put(sc, tk, done["qn"], *ss[0].free, *ss[1].free)
                for h in range(8):
                    bsl = bound_rel(qb, h)[:, 31:31 + 16 * (n - 1) + 1:16]
                    tv = V.put(lambda e, h=h, n=n, bsl=bsl, mx=mx, ss=ss: e.tensor_tensor_reduce(
                        Pc[:, h, 0:n], ss[h // 4].ap[:, 16 * (h % 4):16 * (h % 4) + n], bsl, 1.0, -3.0e38,
                        ALU.add, ALU.max, mx[:, h:h + 1]), tp, *done["rel"], *([tco] if tco else []))
                ss[0].free = ss[1].free = [tv]
                te = softmax_block(Pc, mx, sums, 8, n, [tv])
                tr = V.put(lambda e, rec=rec, sums=sums: e.reciprocal(rec, sums), te)
                co = small(8)
                tr = V.put(lambda e, co=co, rec=rec, qb=qb: e.tensor_tensor(co, rec, gf[:, qb, 8:16], ALU.mult), tr, done["gf"])
                if qb == 0:
                    tr = V.put(lambda e, co=co: e.tensor_scalar(co, co, cst[:, C_ROW:C_ROW + 1], None, ALU.mult), tr, t_rest)
                yield
                sl = [SR.get(), SR.get()]

                def tr8(e, sl=sl, n=n):
                    for h in range(8):
                        r = e.transpose(sl[h // 4].ap[0:n, 128 * (h % 4):128 * (h % 4) + 128], Pc[:, h, 0:n], ident)
                    return r

                tp = P.put(tr8, te, *sl[0].free, *sl[1].free)
                for i in range(2):
                    tc = V.put(lambda e, i=i, sl=sl, n=n: e.tensor_copy(
                        PcT[0:n, 4 * i:4 * i + 4, :], sl[i].ap[0:n, :].rearrange("p (h t) -> p h t", h=4)), tp)
                    sl[i].free = [tc]
                tco = tp
                yield
                s = SR.get()

                def pv(e, s=s, n=n):
                    for h in range(8):
                        r = e.matmul(s.ap[:, 64 * h:64 * h + 64], PcT[0:n, h, :], vc[0:n, h // 4, :], start=True, stop=True)
                    return r

                tp = P.put(pv, tc, tk, *s.free)
                o = onsa[:, qb, :].rearrange("p (h d) -> p h d", h=8)
                done["onsa", qb] = V.put(lambda e, o=o, s=s, co=co: e.tensor_tensor(
                    o, s.ap[:, :].rearrange("p (h d) -> p h d", h=8), spread(co, 64), ALU.mult), tp, tr)
                s.free = [done["onsa", qb]]
                yield
            while t_fox in tasks:
                yield
            for w in range(2):
                def score(e, ps, h, qb, L, w=w):
                    pa, ti = tile_of(h)
                    return e.matmul(ps, qn[pa, ti, 128 * qb:128 * qb + 128], ksw[pa, w, 0:L], start=True, stop=True)

                def out(qb, ps, rec, after, w=w):
                    co = small(8)
                    o = onsa[:, qb, :].rearrange("p (h d) -> p h d", h=8)
                    t = V.put(lambda e: e.tensor_tensor(co, rec, gf[:, qb, 16 + 8 * w:24 + 8 * w], ALU.mult), *after, done["gf"])
                    a = V.put(lambda e: e.tensor_tensor(otmp[:, :, :], ps, spread(co, 64), ALU.mult), t)
                    done["onsa", qb] = V.put(lambda e: e.tensor_tensor(o, o, otmp[:, :, :], ALU.add), a, done["onsa", qb])
                    return [a]

                yield from attention(Pb2, PT2, score, bound_rel,
                                      lambda h, k, w=w: vsw[:, k, 128 * w + 64 * (h // 4):128 * w + 64 * (h // 4) + 64],
                                      [done["qn"], done["ksw"], *done["rel"]], [done["vsw"]], out, [P.last], range(8))
        us = Split(u_hi, u_lo, 0, 8)
        yT = Split(u_hi, u_lo, 0, 8)

        def fox():
            bf = cols[0:8, COLS["mix_b_forget_2"][0]:COLS["mix_b_forget_2"][0] + 1]
            z = gfT[0:8, :]
            ta = A.put(lambda e: e.activation(fx[0:8, 0, :], z, ACT.Abs, bias=bf), done["gfT"], t_cols, *done["rel"])
            tv = V.put(lambda e: e.tensor_scalar(fx[0:8, 1, :], z, bf, 0.0, ALU.add, ALU.min), ta, t_cols)
            ta = A.put(lambda e: e.activation(fx[0:8, 0, :], fx[0:8, 0, :], ACT.Exp, scale=-1.0), ta)
            ta = A.put(lambda e: e.activation(fx[0:8, 0, :], fx[0:8, 0, :], ACT.Ln, bias=1.0), ta)
            tv = V.put(lambda e: e.tensor_tensor(fx[0:8, 1, :], fx[0:8, 1, :], fx[0:8, 0, :], ALU.subtract), ta, tv)
            to = V.put(lambda e: e.memset(fx[0:8, 0, :], 1.0), tv)
            tc = V.put(lambda e: e.tensor_tensor_scan(fx[0:8, 2, :], fx[0:8, 0, :], fx[0:8, 1, :], 0.0,
                                                      ALU.mult, ALU.add), tv, to)
            yield

            def score(e, ps, h, qb, L):
                pa = slice(64 * (h % 2), 64 * (h % 2) + 64)
                e.matmul(ps, qf[pa, h // 2, 128 * qb:128 * qb + 128], kf[pa, h // 2, 0:L], start=True, stop=False)
                return e.matmul(ps, sel[0:8, h, :], fx[0:8, 2, 0:L], start=False, stop=True)

            def bias(qb, h):
                o, L = (0, 128) if qb == 0 else (128, 256)
                return cst[:, C_CM + o:C_CM + o + L]

            def out(qb, ps, rec, after):
                o = ofox[:, qb, :].rearrange("p (h d) -> p h d", h=8)
                done["ofox"] = V.put(lambda e: e.tensor_tensor(o, ps, spread(rec, 64), ALU.mult), *after)
                return [done["ofox"]]

            yield from attention(Pb2, PT2, score, bias, lambda h, k: vf[:, k, 64 * h:64 * h + 64],
                                 [done["qf"], done["kf"], tc, t_sel], [done["vf"]], out, [P.last, A.last])
        gemm_b("qf", hT, keep_b("qf", qf, nm_m2, 0.125), {1: lambda: start(left)})
        for q in (A, V):
            q.wait(here)
        gemm_b("kf", hT, keep_b("kf", kf, nm_m2))
        gemm_a("vf", hT, evac_tm("vf", vf, nm_m2))

        def evac_gf(ps, tp):
            done["gfT"] = V.put(lambda e: e.tensor_tensor(gfT[0:32, :], ps, nm_m2.rT[0:32, :], ALU.mult), tp, nm_m2.trT)
            return [done["gfT"]]

        def gf_tokens():
            yield
            s = SR.get()

            def tr(e):
                for t in range(2):
                    r = e.transpose(s.ap[:, 32 * t:32 * t + 32], gfT[0:32, 128 * t:128 * t + 128], ident[0:32, 0:32])
                return r

            tp = P.put(tr, done["gfT"], *s.free)
            done["gf"] = A.put(lambda e: e.activation(gf[:, :, :], s.ap[:, 0:64].rearrange("p (t c) -> p t c", t=2),
                                                      ACT.Sigmoid), tp)
            s.free = [done["gf"]]

        gemm_s("gf", hT, evac_gf)
        spawn(gf_tokens())
        drain(t_memory)
        t_fox = spawn(fox())
        gemm_b("kv", hT, evac_kv)
        gemm_b("qn", hT, keep_b("qn", qn, nm_m2, 0.125))

        def evac_ksw(i, ps, tp):
            p2 = ps[:, :].rearrange("p (i t) -> p i t", i=2)
            done["ksw"] = V.put(lambda e: e.tensor_tensor(ksw[:, :, :], p2, nm_m2.wide(), ALU.mult), tp, nm_m2.trT)
            return [done["ksw"]]

        gemm_b("ksw", hT, evac_ksw)

        gemm_a("vsw", hT, evac_tm("vsw", vsw, nm_m2))

        t_nsa = spawn(nsa())
        ggt = {}
        for n in range(4):
            def evac(t, ps, tp, n=n):
                ggt[n, t] = A.put(lambda e: e.activation(gg[:, t, 512 * n:512 * n + 512], ps[:, :], ACT.Sigmoid,
                                                          scale=nm_m2.r[:, t:t + 1]), tp, nm_m2.tr)
                return [ggt[n, t]]
            gemm_a(f"gg{n}", hT, evac)
        drain(t_fox)
        for n in range(2):
            gemm_b(f"mkv{n}", mT, keep_b("ckT", ckT[:, 4 * n:4 * n + 4, :], nm_mk))
        for n in range(2):
            gemm_a(f"mkv{2 + n}", mT, evac_tm("cv", cv[:, :, 512 * n:512 * n + 512], nm_mk))
        to_split(us, 0, 4, lambda t: ofox[:, t, :], [done["ofox"]])
        yt = {}

        def y_first():
            yield
            to_split(yT, 0, 4, lambda t: y2[:, t, 0:512], [yt[0, 0], yt[1, 0]])

        for i in (1, 0):
            sub = Split(u_hi, u_lo, 4 * (1 - i), 4)
            if i == 0:
                drain(t_nsa)
                to_split(us, 4, 4, lambda t: onsa[:, t, :], [done["onsa", 0], done["onsa", 1]])
            sub.tok = us.tok[4 * (1 - i):4 * (1 - i) + 4]
            for n in range(2):
                def evac(t, ps, tp, n=n, i=i):
                    gsl = gg[:, t, 1024 * i + 512 * n:1024 * i + 512 * n + 512]
                    yy = y2[:, t, 512 * n:512 * n + 512]
                    if i == 1:
                        yt[t, n] = V.put(lambda e: e.tensor_tensor(yy, ps[:, :], gsl, ALU.mult), tp, ggt[2 * i + n, t])
                        return [yt[t, n]]
                    a = V.put(lambda e: e.tensor_tensor(ytmp[:, t, :], ps[:, :], gsl, ALU.mult), tp, ggt[2 * i + n, t],
                              *yt.get(("f", t), []))
                    yt[t, n] = V.put(lambda e: e.tensor_tensor(yy, yy, ytmp[:, t, :], ALU.add), a, yt[t, n])
                    yt["f", t] = [yt[t, n]]
                    return [a]
                gemm_a(f"up{i}{n}", sub, evac)
                if (i, n) == (0, 0):
                    spawn(y_first())
        drain()
        cm = Phase("cm")
        cm.new("memory", [128, 4, D])
        oT_hi, oT_lo = cm.new("oT_hi", [128, 8, T], F32R), cm.new("oT_lo", [128, 8, T], F32R)
        cm.new("past_y", [128, 2, D])
        cqT = cm.new("cqT", [128, 8, T])
        cP = cm.new("cP", [128, 2, 4, T])
        cPT = cm.new("cPT", [128, 2, 8, 128])
        co = cm.new("co", [128, 2, D])
        oT = Split(oT_hi, oT_lo, 0, 8)
        here = everything()
        nm_cq = Norm(5, "mem_q_norm_2", hT, x)
        nm_f2 = Norm(6, "ffn2_norm_2", hT, x)

        def y_second():
            to_split(yT, 4, 4, lambda t: y2[:, t, 512:1024], [yt[0, 1], yt[1, 1]])

        x_tok, left = residual("mo", yT, 1.0, x_tok, nm_cq, {2: y_second})
        for q in (A, V):
            q.wait(here)
        def mem_heads(g):
            rec, te, tc, tv = [None, None], [None, None], [None, None], [None, None]
            for qb in range(2):
                mx, sums, rec[qb] = small(2), small(2), small(2)
                s = SR.get()

                def sc(e, s=s, qb=qb):
                    for i in range(2):
                        for k in range(2):
                            f = 2 * (2 * g + i) + k
                            r = e.matmul(s.ap[:, 256 * i:256 * i + 256], cqT[:, f, 128 * qb:128 * qb + 128], ckT[:, f, :],
                                         start=k == 0, stop=k == 1)
                    return r

                tp = P.put(sc, done["cqT", g], done["ckT"], *s.free)
                p2 = s.ap[:, :].rearrange("p (i t) -> p i t", i=2)
                t = V.put(lambda e, p2=p2, mx=mx: e.tensor_reduce(mx, p2, AX, ALU.max), tp)
                t = V.put(lambda e, mx=mx: e.tensor_scalar(mx, mx, -1.0, None, ALU.mult), t)
                for i in range(2):
                    te[qb] = A.put(lambda e, p2=p2, i=i, qb=qb, mx=mx, sums=sums: e.activation(
                        cP[:, qb, 2 * g + i, :], p2[:, i, :], ACT.Exp, bias=mx[:, i:i + 1], accum_out=sums[:, i:i + 1]), t)
                s.free = [te[qb]]
                rec[qb] = (rec[qb], V.put(lambda e, r=rec[qb], sums=sums: e.reciprocal(r, sums), te[qb]))
            yield
            for qb in range(2):
                s = SR.get()

                def tr4(e, s=s, qb=qb):
                    for i in range(4):
                        r = e.transpose(s.ap[:, 128 * i:128 * i + 128],
                                        cP[:, qb, 2 * g + i // 2, 128 * (i % 2):128 * (i % 2) + 128], ident)
                    return r

                tp = P.put(tr4, te[qb], *s.free)
                o, p4 = cPT[:, qb, 4 * g:4 * g + 4, :], s.ap[:, :].rearrange("p (i t) -> p i t", i=4)
                if qb == 0:
                    tc[qb] = V.put(lambda e, o=o, p4=p4: e.tensor_copy(o, p4), tp)
                else:
                    tc[qb] = A.put(lambda e, o=o, p4=p4: e.activation(o, p4, ACT.Copy), tp)
                s.free = [tc[qb]]
            yield
            for qb in range(2):
                s = SR.get()

                def pv(e, s=s, qb=qb):
                    for i in range(2):
                        h = 2 * g + i
                        for k in range(2):
                            r = e.matmul(s.ap[:, 256 * i:256 * i + 256], cPT[:, qb, 2 * h + k, :],
                                         cv[:, k, 256 * h:256 * h + 256], start=k == 0, stop=k == 1)
                    return r

                tp = P.put(pv, tc[qb], done["cv"], *s.free)
                o = co[:, qb, 512 * g:512 * g + 512].rearrange("p (i d) -> p i d", i=2)
                r, tr = rec[qb]
                tv[qb] = V.put(lambda e, s=s, o=o, r=r: e.tensor_tensor(
                    o, s.ap[:, :].rearrange("p (i d) -> p i d", i=2), spread(r, 256), ALU.mult), tp, tr)
                s.free = [tv[qb]]
            yield
            to_split(oT, 4 * g, 4, lambda t: co[:, t, 512 * g:512 * g + 512], tv)

        for g in range(2):
            gemm_b(f"cq{g}", hT, keep_b("cqT", cqT[:, 4 * g:4 * g + 4, :], nm_cq, 1.0 / 16),
                   {} if g else {1: lambda: start(left)})
            done["cqT", g] = done["cqT"]
            heads = mem_heads(g)
            spawn(heads)
            if g:
                drain(*[t for t in tasks if t is not heads])
        x_tok, left = residual("co", oT, 1.0, x_tok, nm_f2, {2: drain})

        t_row3 = load(SP, "row3", row[:, :], bcast(io["final_norm_2"], D), *early)
        ph = Phase("end")
        xe = ph.new("xe", [128, 2, D])
        xrow = ph.new("xrow", [128, 2, 512], off=m2_late)
        es, e2, er = small(4), small(2), small(2)
        etok = {}

        def last_sums(n, toks):
            for t in range(2):
                etok[n] = A.put(lambda e, t=t: e.activation(
                    junk[:, :], x[:, t, 512 * n:512 * n + 512], ACT.Square, accum_out=es[:, 2 * n + t:2 * n + t + 1]),
                    toks[t], *junk_tok)
                junk_tok[:] = [etok[n]]

        def fin2(name, hid, fb, mid):
            out = [None, None]

            def first_half(toks):
                yield
                last_sums(0, toks)
                for t in range(2):
                    etok["row"] = V.put(lambda e, t=t: e.tensor_tensor(xrow[:, t, :], x[:, t, 0:512], row[:, 0:512],
                                                                       ALU.mult), toks[t], t_row3)

            for n in range(2):
                def evac(t, ps, tp, n=n):
                    xx = x[:, t, 512 * n:512 * n + 512]
                    out[t] = V.put(lambda e: e.scalar_tensor_tensor(
                        out=xx, in0=ps[:, :], scalar=0.5, in1=xx, op0=ALU.mult, op1=ALU.add), tp, x_tok[t])
                    return [out[t]]
                gemm_a(f"{name}{n}", hid, evac, mid if n == 0 else {})
                if n == 0:
                    spawn(first_half(list(out)))
            last_sums(1, out)
            return out

        x_tok = ffn("f2", nm_f2, {1: lambda: start(left)}, fin2)
        t = V.put(lambda e: e.tensor_tensor(e2, es[:, 0:2], es[:, 2:4], ALU.add), etok[0], etok[1])
        tr = rstd(er, e2, 2, 1.0 / D, t)
        oo = io["out"].rearrange("a (k p) d -> p (a k) d", p=128)
        A.wait([P.last])
        V.wait([P.last])
        t_out = []
        for t in range(2):
            a = A.put(lambda e, t=t: e.activation(xe[:, t, 0:512], xrow[:, t, :], ACT.Identity, scale=er[:, t:t + 1]),
                      tr, etok["row"])
            v = V.put(lambda e, t=t: e.scalar_tensor_tensor(
                out=xe[:, t, 512:1024], in0=x[:, t, 512:1024], scalar=er[:, t:t + 1], in1=row[:, 512:1024],
                op0=ALU.mult, op1=ALU.mult), tr, t_row3)
            t_out.append(SP.put(s_out, cnt, oo[:, t, :], xe[:, t, :], a, v))
        assert nxt[0] == len(units)

        block = ctx.enter_context(nc.Block())

        @block.sync
        def _(eng):
            SP.run(eng)
            eng.wait_ge(*t_out[-1])

        @block.scalar
        def _(eng):
            AD.run(eng)
            A.run(eng)

        @block.vector
        def _(eng):
            V.run(eng)

        @block.tensor
        def _(eng):
            P.run(eng)

        @block.gpsimd
        def _(eng):
            G.run(eng)


_RAW = ["x", "gla_w_g2", "pool_w", "gla_norm", "norm_mix_post", "norm_ffn_post", "mem_2", "rel_bias_table_2",
        "cmp_pos_k_2", "cmp_pos_v_2", "cmp_k_w1_2", "cmp_k_w2_2", "cmp_v_w1_2", "cmp_v_w2_2", "final_norm_2"]


def lay_out(inputs):
    arrays = {n: np.ascontiguousarray(inputs[n]) for n in _RAW}
    units, chunks, total = unit_plan()
    flat = np.empty(total, np.float32)
    for name, weight, cols, rows in weight_chunks():
        ws = weight if isinstance(weight, tuple) else (weight,)
        w = np.concatenate([np.asarray(inputs[n])[0][:, cols] for n in ws], 1)
        for u in chunks[name]:
            off, k, n, k0 = units[u]
            part = w[128 * k0:128 * (k0 + k)].reshape(k, 128, n).transpose(1, 0, 2)
            flat[off:off + 128 * k * n] = part.reshape(-1)
    arrays["wflat"] = flat
    cols = np.zeros((128, N_COLS), np.float32)
    for name, (c, w) in COLS.items():
        v = np.asarray(inputs[name]).reshape(-1)
        if len(v) == 8:
            cols[0:8, c] = v
        else:
            cols[:, c:c + w] = v.reshape(w, 128).T
    arrays["cols"] = cols
    arrays.update(constants())
    return arrays


def kernel(**inputs):
    import concourse.bacc as bacc
    from concourse.bass_utils import run_bass_kernel_spmd

    nc = bacc.Bacc("TRN2", target_bir_lowering=False, num_devices=1)
    arrays = {f"in_{n}": a for n, a in lay_out(inputs).items()}
    io = {n[3:]: nc.dram_tensor(n, a.shape, mybir.dt.from_np(a.dtype), kind="ExternalInput").ap()
          for n, a in arrays.items()}
    io["out"] = nc.dram_tensor("out", (1, T, D), F32, kind="ExternalOutput").ap()
    build(nc, io)
    r = run_bass_kernel_spmd(nc, [arrays], core_ids=[0])
    return r.results[0]["out"]
```
